# Optimizing a Trainium2 kernel written in Bass

```python
import math
import jax, jax.numpy as jnp
from jax import lax
import numpy as np

D_MODEL = 1024
BATCH = 1
SEQ = 256
DEPTH = 2

Q_BLOCK = 128
NEG_INF = -1e30
FORCE_SEL = 1e9
EPS = 1e-6

NSA_HEADS = 8
NSA_KV_GROUPS = 2
NSA_HPG = NSA_HEADS // NSA_KV_GROUPS
NSA_HEAD_DIM = 64
CMP_LEN = 32
CMP_STRIDE = 16
CMP_RATIO = CMP_LEN // CMP_STRIDE
CMP_HIDDEN = 128
SLC_BLOCK = 64
SLC_RATIO = SLC_BLOCK // CMP_STRIDE
SLC_TOPK = 16
SLC_LOCAL = 2
WINDOW = 512

MLA_HEADS = 8
MLA_Q_RANK = 256
MLA_KV_RANK = 128
MLA_NOPE_DIM = 64
MLA_ROPE_DIM = 32
MLA_QK_DIM = MLA_NOPE_DIM + MLA_ROPE_DIM
MLA_V_DIM = 64
ROPE_THETA = 10000.0

FOX_HEADS = 8
FOX_HEAD_DIM = 64

REL_BUCKETS = 32
REL_MAX_DIST = 128

N_BRANCHES = 3
N_GROUPS = 4
EXPERTS_PER_GROUP = 8
N_EXPERTS = N_GROUPS * EXPERTS_PER_GROUP
TOP_K_IN_GROUP = 2
EXPERT_DIM = 256
MOE_CHUNK = 128

NSA_Q_W = NSA_HEADS * NSA_HEAD_DIM
NSA_KV_W = 3 * 2 * NSA_KV_GROUPS * NSA_HEAD_DIM
NSA_G_W = 3 * NSA_HEADS
FOX_QKV_W = 3 * FOX_HEADS * FOX_HEAD_DIM
MERGE_W = N_BRANCHES * D_MODEL
IN_SPLITS = (NSA_Q_W, NSA_KV_W, NSA_G_W, MLA_Q_RANK, MLA_KV_RANK, MLA_ROPE_DIM, FOX_QKV_W, FOX_HEADS, MERGE_W)
D_IN = sum(IN_SPLITS)

kernel_name = "hybrid_nsa_mla_fox_hmoe"

def rmsnorm(x, g):
    xf = x.astype(jnp.float32)
    y = xf * lax.rsqrt(jnp.mean(xf * xf, axis=-1, keepdims=True) + EPS)
    return (y * g.astype(jnp.float32)).astype(x.dtype)

def rel_bucket(dist):
    n = jnp.maximum(dist, 0)
    max_exact = REL_BUCKETS // 2
    log_ratio = jnp.log(jnp.maximum(n, 1).astype(jnp.float32) / max_exact) / math.log(REL_MAX_DIST / max_exact)
    large = max_exact + (log_ratio * (REL_BUCKETS - max_exact)).astype(jnp.int32)
    return jnp.where(n < max_exact, n, jnp.minimum(large, REL_BUCKETS - 1))

def rope(x, pos):
    half = x.shape[-1] // 2
    inv_freq = ROPE_THETA ** (-jnp.arange(half, dtype=jnp.float32) / half)
    ang = pos.astype(jnp.float32)[..., None] * inv_freq
    ang = ang.reshape(ang.shape[:2] + (1,) * (x.ndim - 3) + (half,))
    cos, sin = jnp.cos(ang), jnp.sin(ang)
    x1 = x[..., :half].astype(jnp.float32)
    x2 = x[..., half:].astype(jnp.float32)
    return jnp.concatenate([x1 * cos - x2 * sin, x1 * sin + x2 * cos], axis=-1).astype(x.dtype)

def compress_blocks(raw, pe, w1, b1, w2):
    B, T, G, dh = raw.shape
    n_sub = T // CMP_STRIDE
    sub = raw.reshape(B, n_sub, CMP_STRIDE, G, dh)
    blocks = jnp.concatenate([sub[:, r:n_sub - CMP_RATIO + 1 + r] for r in range(CMP_RATIO)], axis=2)
    blocks = blocks + pe[None, None, :, None, :]
    flat = blocks.transpose(0, 1, 3, 2, 4).reshape(B, n_sub - CMP_RATIO + 1, G, CMP_LEN * dh)
    return jax.nn.gelu(flat @ w1 + b1) @ w2

def causal_block_attention(q, k, v, scale, cum_log_f=None):
    B, T, H, _ = q.shape
    kpos = jnp.arange(T)
    cum_k = None if cum_log_f is None else cum_log_f.transpose(0, 2, 1)[:, :, None, :]

    def one_block(qb):
        t0 = qb * Q_BLOCK
        qpos = t0 + jnp.arange(Q_BLOCK)
        q_blk = lax.dynamic_slice_in_dim(q, t0, Q_BLOCK, axis=1)
        s = jnp.einsum('bqhd,bkhd->bhqk', q_blk, k, preferred_element_type=jnp.float32) * scale
        if cum_log_f is not None:
            cum_q = lax.dynamic_slice_in_dim(cum_log_f, t0, Q_BLOCK, axis=1).transpose(0, 2, 1)[..., None]
            s = s + cum_q - cum_k
        s = jnp.where(kpos[None, :] <= qpos[:, None], s, NEG_INF)
        p = jax.nn.softmax(s, axis=-1).astype(v.dtype)
        return jnp.einsum('bhqk,bkhd->bqhd', p, v)

    out = lax.map(one_block, jnp.arange(T // Q_BLOCK))
    return out.transpose(1, 0, 2, 3, 4).reshape(B, T, H, v.shape[-1])

def nsa_attention(q, kc_raw, vc_raw, ks, vs, kw, vw, gate_logits, rel_bias, pe,
                  ck_w1, ck_b1, ck_w2, cv_w1, cv_b1, cv_w2):
    B, T, H, dh = q.shape
    G, HPG = NSA_KV_GROUPS, NSA_HPG
    scale = dh ** -0.5
    kc = compress_blocks(kc_raw, pe, ck_w1, ck_b1, ck_w2)
    vc = compress_blocks(vc_raw, pe, cv_w1, cv_b1, cv_w2)
    n_cmp = kc.shape[1]
    cmp_end = jnp.arange(n_cmp) * CMP_STRIDE + CMP_LEN - 1
    n_slc = T // SLC_BLOCK
    ks_blk = ks.reshape(B, n_slc, SLC_BLOCK, G, dh).transpose(0, 3, 1, 2, 4)
    vs_blk = vs.reshape(B, n_slc, SLC_BLOCK, G, dh).transpose(0, 3, 1, 2, 4)
    topk = min(SLC_TOPK, n_slc)
    max_start = SLC_RATIO + CMP_RATIO - 2
    right_pad = max(0, max_start + SLC_RATIO * (n_slc - 1) + 1 - n_cmp)
    kw_pad = jnp.pad(kw, ((0, 0), (WINDOW, 0), (0, 0), (0, 0)))
    vw_pad = jnp.pad(vw, ((0, 0), (WINDOW, 0), (0, 0), (0, 0)))
    gates = jax.nn.sigmoid(gate_logits.astype(jnp.float32))
    tab_g = rel_bias.reshape(REL_BUCKETS, G, HPG)
    n_win = WINDOW + Q_BLOCK

    def one_block(qb):
        t0 = qb * Q_BLOCK
        tq = t0 + jnp.arange(Q_BLOCK)
        qg = lax.dynamic_slice_in_dim(q, t0, Q_BLOCK, axis=1).reshape(B, Q_BLOCK, G, HPG, dh)

        dist_c = tq[:, None] - cmp_end[None, :]
        ok_c = dist_c >= 0
        bias_c = rel_bias[rel_bucket(dist_c)].reshape(Q_BLOCK, n_cmp, G, HPG).transpose(2, 3, 0, 1)
        s_c = jnp.einsum('bqghd,bngd->bghqn', qg, kc, preferred_element_type=jnp.float32) * scale + bias_c
        s_c = jnp.where(ok_c, s_c, NEG_INF)
        p_c = jnp.where(ok_c, jax.nn.softmax(s_c, axis=-1), 0.0)
        o_c = jnp.einsum('bghqn,bngd->bqghd', p_c.astype(vc.dtype), vc)

        imp = jnp.pad(p_c.sum(axis=2), ((0, 0), (0, 0), (0, 0), (0, right_pad)))
        p_slc = jnp.zeros(imp.shape[:3] + (n_slc,), jnp.float32)
        for m in range(SLC_RATIO):
            for n in range(CMP_RATIO):
                st = m + n
                p_slc = p_slc + lax.slice_in_dim(imp, st, st + SLC_RATIO * (n_slc - 1) + 1, stride=SLC_RATIO, axis=3)
        blk_cur = tq // SLC_BLOCK
        j = jnp.arange(n_slc)
        causal_b = j[None, :] <= blk_cur[:, None]
        forced = (j[None, :] == 0) | (causal_b & (j[None, :] > blk_cur[:, None] - SLC_LOCAL))
        score = jnp.where(causal_b, jnp.where(forced, FORCE_SEL, p_slc), NEG_INF)
        _, idx = lax.top_k(score, topk)
        sel_ok = idx <= blk_cur[None, None, :, None]
        flat_idx = idx.reshape(B, G, Q_BLOCK * topk)[..., None, None]
        k_sel = jnp.take_along_axis(ks_blk, flat_idx, axis=2).reshape(B, G, Q_BLOCK, topk * SLC_BLOCK, dh)
        v_sel = jnp.take_along_axis(vs_blk, flat_idx, axis=2).reshape(B, G, Q_BLOCK, topk * SLC_BLOCK, dh)
        kpos_s = idx[..., None] * SLC_BLOCK + jnp.arange(SLC_BLOCK)
        ok_s = ((kpos_s <= tq[None, None, :, None, None]) & sel_ok[..., None]).reshape(B, G, Q_BLOCK, -1)
        dist_s = tq[None, None, :, None] - kpos_s.reshape(B, G, Q_BLOCK, -1)
        bias_s = jax.vmap(lambda tb, bk: tb[bk], in_axes=(1, 1), out_axes=1)(tab_g, rel_bucket(dist_s))
        bias_s = bias_s.transpose(0, 1, 4, 2, 3)
        s_s = jnp.einsum('bqghd,bgqkd->bghqk', qg, k_sel, preferred_element_type=jnp.float32) * scale + bias_s
        s_s = jnp.where(ok_s[:, :, None], s_s, NEG_INF)
        p_s = jax.nn.softmax(s_s, axis=-1).astype(v_sel.dtype)
        o_s = jnp.einsum('bghqk,bgqkd->bqghd', p_s, v_sel)

        k_win = lax.dynamic_slice_in_dim(kw_pad, t0, n_win, axis=1)
        v_win = lax.dynamic_slice_in_dim(vw_pad, t0, n_win, axis=1)
        kpos_w = t0 - WINDOW + jnp.arange(n_win)
        dist_w = tq[:, None] - kpos_w[None, :]
        ok_w = (dist_w >= 0) & (dist_w < WINDOW) & (kpos_w[None, :] >= 0)
        bias_w = rel_bias[rel_bucket(dist_w)].reshape(Q_BLOCK, n_win, G, HPG).transpose(2, 3, 0, 1)
        s_w = jnp.einsum('bqghd,bkgd->bghqk', qg, k_win, preferred_element_type=jnp.float32) * scale + bias_w
        s_w = jnp.where(ok_w, s_w, NEG_INF)
        p_w = jax.nn.softmax(s_w, axis=-1).astype(v_win.dtype)
        o_w = jnp.einsum('bghqk,bkgd->bqghd', p_w, v_win)

        g = lax.dynamic_slice_in_dim(gates, t0, Q_BLOCK, axis=1).reshape(B, Q_BLOCK, G, HPG, 3)
        out = g[..., 0:1] * o_c + g[..., 1:2] * o_s + g[..., 2:3] * o_w
        return out.reshape(B, Q_BLOCK, H * dh).astype(q.dtype)

    out = lax.map(one_block, jnp.arange(T // Q_BLOCK))
    return out.transpose(1, 0, 2, 3).reshape(B, T, H * dh)

def hier_moe(h, w_grp, b_grp, w_router, b_router, w_gate, w_up, w_down):
    B, T, D = h.shape
    tok = h.reshape(-1, MOE_CHUNK, D)

    def chunk(t):
        grp_p = jax.nn.softmax((t @ w_grp).astype(jnp.float32) + b_grp.astype(jnp.float32), axis=-1)
        grp_top, g_idx = lax.top_k(grp_p, 1)
        e_logit = ((t @ w_router).astype(jnp.float32) + b_router.astype(jnp.float32)).reshape(-1, N_GROUPS, EXPERTS_PER_GROUP)
        e_logit = jnp.take_along_axis(e_logit, g_idx[:, :, None], axis=1)[:, 0]
        e_p = jax.nn.softmax(e_logit, axis=-1)
        e_top, e_idx = lax.top_k(e_p, TOP_K_IN_GROUP)
        wts = grp_top * e_top / jnp.sum(e_top, axis=-1, keepdims=True)
        eid = g_idx * EXPERTS_PER_GROUP + e_idx
        combine = jnp.sum(jax.nn.one_hot(eid, N_EXPERTS, dtype=jnp.float32) * wts[..., None], axis=1)
        a = jnp.einsum('cd,edf->cef', t, w_gate)
        u = jnp.einsum('cd,edf->cef', t, w_up)
        hid = (jax.nn.silu(a) * u * combine[..., None]).astype(t.dtype)
        return jnp.einsum('cef,efd->cd', hid, w_down)

    return lax.map(chunk, tok).reshape(B, T, D)

def setup_inputs(seed: int = 0) -> dict:
    key = jax.random.key(seed)
    ks = jax.random.split(key, 48)
    counter = [0]

    def nk():
        counter[0] += 1
        return ks[counter[0] - 1]

    def nrm(shape, scale):
        return jax.random.normal(nk(), shape, jnp.float32) * scale

    def gain(shape):
        return 1.0 + nrm(shape, 0.02)

    L, D = DEPTH, D_MODEL
    cmp_in = CMP_LEN * NSA_HEAD_DIM
    x = nrm((BATCH, SEQ, D), 1.0)
    offset = jax.random.randint(nk(), (BATCH, 1), 0, 1024, dtype=jnp.int32)
    positions = offset + jnp.arange(SEQ, dtype=jnp.int32)[None, :]
    return {
        "x": x,
        "positions": positions,
        "rel_bias": nrm((REL_BUCKETS, NSA_HEADS), 0.5),
        "norm_attn": gain((L, D)),
        "w_in": nrm((L, D, D_IN), D ** -0.5),
        "b_merge": nrm((L, MERGE_W), 0.1),
        "cmp_pe": nrm((L, CMP_LEN, NSA_HEAD_DIM), 0.1),
        "cmp_k_w1": nrm((L, cmp_in, CMP_HIDDEN), cmp_in ** -0.5),
        "cmp_k_b1": nrm((L, CMP_HIDDEN), 0.02),
        "cmp_k_w2": nrm((L, CMP_HIDDEN, NSA_HEAD_DIM), CMP_HIDDEN ** -0.5),
        "cmp_v_w1": nrm((L, cmp_in, CMP_HIDDEN), cmp_in ** -0.5),
        "cmp_v_b1": nrm((L, CMP_HIDDEN), 0.02),
        "cmp_v_w2": nrm((L, CMP_HIDDEN, NSA_HEAD_DIM), CMP_HIDDEN ** -0.5),
        "mla_q_norm": gain((L, MLA_Q_RANK)),
        "mla_kv_norm": gain((L, MLA_KV_RANK)),
        "mla_w_uq": nrm((L, MLA_Q_RANK, MLA_HEADS * MLA_QK_DIM), MLA_Q_RANK ** -0.5),
        "mla_w_uk": nrm((L, MLA_KV_RANK, MLA_HEADS * MLA_NOPE_DIM), MLA_KV_RANK ** -0.5),
        "mla_w_uv": nrm((L, MLA_KV_RANK, MLA_HEADS * MLA_V_DIM), MLA_KV_RANK ** -0.5),
        "fox_b_f": jax.random.uniform(nk(), (L, FOX_HEADS), jnp.float32, 1.0, 4.0),
        "w_o_nsa": nrm((L, NSA_HEADS * NSA_HEAD_DIM, D), (NSA_HEADS * NSA_HEAD_DIM) ** -0.5),
        "w_o_mla": nrm((L, MLA_HEADS * MLA_V_DIM, D), (MLA_HEADS * MLA_V_DIM) ** -0.5),
        "w_o_fox": nrm((L, FOX_HEADS * FOX_HEAD_DIM, D), (FOX_HEADS * FOX_HEAD_DIM) ** -0.5),
        "w_out": nrm((L, D, D), D ** -0.5),
        "norm_ffn": gain((L, D)),
        "moe_w_grp": nrm((L, D, N_GROUPS), D ** -0.5),
        "moe_b_grp": nrm((L, N_GROUPS), 0.01),
        "moe_w_router": nrm((L, D, N_EXPERTS), D ** -0.5),
        "moe_b_router": nrm((L, N_EXPERTS), 0.01),
        "moe_w_gate": nrm((L, N_EXPERTS, D, EXPERT_DIM), D ** -0.5),
        "moe_w_up": nrm((L, N_EXPERTS, D, EXPERT_DIM), D ** -0.5),
        "moe_w_down": nrm((L, N_EXPERTS, EXPERT_DIM, D), EXPERT_DIM ** -0.5),
        "norm_final": gain((D,)),
    }

def reference(x, positions, rel_bias, norm_attn, w_in, b_merge, cmp_pe, cmp_k_w1, cmp_k_b1, cmp_k_w2,
              cmp_v_w1, cmp_v_b1, cmp_v_w2, mla_q_norm, mla_kv_norm, mla_w_uq, mla_w_uk, mla_w_uv, fox_b_f,
              w_o_nsa, w_o_mla, w_o_fox, w_out, norm_ffn, moe_w_grp, moe_b_grp, moe_w_router, moe_b_router,
              moe_w_gate, moe_w_up, moe_w_down, norm_final):
    B, T, D = x.shape
    split_points = [int(c) for c in np.cumsum(IN_SPLITS)[:-1]]
    for l in range(DEPTH):
        h = rmsnorm(x, norm_attn[l])
        proj = h @ w_in[l]
        nsa_q, nsa_kv, nsa_g, mla_cq, mla_ckv, mla_kr, fox_qkv, fox_f, merge_logits = jnp.split(proj, split_points, axis=-1)

        q_a = nsa_q.reshape(B, T, NSA_HEADS, NSA_HEAD_DIM)
        kv_a = nsa_kv.reshape(B, T, 3, 2, NSA_KV_GROUPS, NSA_HEAD_DIM)
        out_a = nsa_attention(q_a, kv_a[:, :, 0, 0], kv_a[:, :, 0, 1], kv_a[:, :, 1, 0], kv_a[:, :, 1, 1],
                              kv_a[:, :, 2, 0], kv_a[:, :, 2, 1], nsa_g.reshape(B, T, NSA_HEADS, 3), rel_bias,
                              cmp_pe[l], cmp_k_w1[l], cmp_k_b1[l], cmp_k_w2[l], cmp_v_w1[l], cmp_v_b1[l], cmp_v_w2[l])

        c_q = rmsnorm(mla_cq, mla_q_norm[l])
        q_b = (c_q @ mla_w_uq[l]).reshape(B, T, MLA_HEADS, MLA_QK_DIM)
        q_b = jnp.concatenate([q_b[..., :MLA_NOPE_DIM], rope(q_b[..., MLA_NOPE_DIM:], positions)], axis=-1)
        c_kv = rmsnorm(mla_ckv, mla_kv_norm[l])
        k_nope = (c_kv @ mla_w_uk[l]).reshape(B, T, MLA_HEADS, MLA_NOPE_DIM)
        v_b = (c_kv @ mla_w_uv[l]).reshape(B, T, MLA_HEADS, MLA_V_DIM)
        k_rope = rope(mla_kr, positions)
        k_b = jnp.concatenate([k_nope, jnp.broadcast_to(k_rope[:, :, None, :], (B, T, MLA_HEADS, MLA_ROPE_DIM))], axis=-1)
        out_b = causal_block_attention(q_b, k_b, v_b, MLA_QK_DIM ** -0.5).reshape(B, T, MLA_HEADS * MLA_V_DIM)

        qkv_c = fox_qkv.reshape(B, T, 3, FOX_HEADS, FOX_HEAD_DIM)
        log_f = jax.nn.log_sigmoid(fox_f.astype(jnp.float32) + fox_b_f[l].astype(jnp.float32))
        cum_log_f = jnp.cumsum(log_f, axis=1)
        out_c = causal_block_attention(qkv_c[:, :, 0], qkv_c[:, :, 1], qkv_c[:, :, 2], FOX_HEAD_DIM ** -0.5,
                                       cum_log_f).reshape(B, T, FOX_HEADS * FOX_HEAD_DIM)

        gates = jax.nn.sigmoid((merge_logits + b_merge[l]).astype(jnp.float32)).reshape(B, T, N_BRANCHES, D)
        mixed = (gates[:, :, 0] * (out_a @ w_o_nsa[l]) + gates[:, :, 1] * (out_b @ w_o_mla[l])
                 + gates[:, :, 2] * (out_c @ w_o_fox[l]))
        x = x + mixed.astype(x.dtype) @ w_out[l]

        x = x + hier_moe(rmsnorm(x, norm_ffn[l]), moe_w_grp[l], moe_b_grp[l], moe_w_router[l], moe_b_router[l],
                         moe_w_gate[l], moe_w_up[l], moe_w_down[l])
    return rmsnorm(x, norm_final)


_drawn_inputs = setup_inputs


def setup_inputs(seed=0):
    import zlib

    import numpy as np

    out = dict(_drawn_inputs(seed))
    spreads = {}
    factors = {'cmp_k_b1': 11.631,
     'cmp_v_b1': 3.642,
     'mla_q_norm': 6.089,
     'moe_b_router': 2.775,
     'norm_final': 8.407,
     'moe_b_grp': 5.255}
    for name, (base, spread) in spreads.items():
        noise = np.random.default_rng([zlib.crc32(name.encode()), seed]).standard_normal(out[name].shape)
        drawn = base * np.exp(spread * noise) if base else spread * noise
        out[name] = __import__('jax').numpy.asarray(drawn.astype(out[name].dtype))
    for name, factor in factors.items():
        out[name] = (out[name] * factor).astype(out[name].dtype)
    return out
```

```python
from contextlib import ExitStack

import numpy as np

import concourse.bass as bass
from concourse import mybir
from concourse.alu_op_type import AluOpType as ALU

F32 = mybir.dt.float32
I32 = mybir.dt.int32
U32 = mybir.dt.uint32
ACT = mybir.ActivationFunctionType
AX = mybir.AxisListType
ENG = mybir.EngineType

P = 128
D = 1024
T = 256
NT = T // P
DEPTH = 2
KD = D // P
EPS = 1e-6
BIG = 1e30

H = 8
DH = 64
NQ = H * DH
QK = 96
ROPE = 32
HALF = ROPE // 2
CMP = 16
NCMP = T // CMP - 1
HID = 128

NE = 32
NG = 4
F = 256
CAP = 32
NGRP = NE // 4
PASSES = T // CAP

SLOTS = 12
SLOT = 2048
ATT_LOADS = 36
LOADS = ATT_LOADS + 12 * NGRP
TURNS = LOADS // SLOTS
assert LOADS % SLOTS == 0 and ATT_LOADS % SLOTS == 0

C_NQ, C_KC, C_KS, C_KW, C_G = 0, 512, 768, 1024, 1280
C_FQ, C_FK, C_FV, C_FF, C_MG = 1720, 2232, 2744, 3256, 3264
M_CQ, M_CKV, M_KR, M_FF, M_W = 24, 280, 408, 440, 448

L_MPA, L_MPB, L_NQ, L_KC, L_KS, L_KW, L_FQ, L_FK, L_FV, L_UQ, L_MRG, L_OUT = 0, 1, 2, 4, 5, 6, 7, 9, 11, 13, 14, 32

K_ID, K_TRI, K_ONES, K_STRICT, K_IOTA, K_HM, K_OK, K_MASK, K_INV, K_GRP, K_W = (
    0, 128, 256, 384, 512, 576, 584, 616, 872, 888, 920)
OH_W = 384


def shape_constants():
    p = np.arange(P)[:, None]
    j = np.arange(P)[None, :]
    c = np.zeros((P, K_W), np.float32)
    c[:, K_ID:K_ID + P] = p == j
    c[:, K_TRI:K_TRI + P] = j >= p
    c[:, K_ONES:K_ONES + P] = 1
    c[:, K_STRICT:K_STRICT + P] = j > p
    c[:, K_IOTA:K_IOTA + CAP] = np.arange(CAP)
    c[:, K_HM:K_HM + H] = (p // 16) == np.arange(H)[None, :]
    n = np.arange(16)[None, :]
    for t in range(NT):
        c[:, K_OK + 16 * t:K_OK + 16 * t + 16] = (t * P + p - (n * CMP + 31) >= 0) & (n < NCMP)
    c[:, K_MASK:K_MASK + T] = np.where(P + p - np.arange(T)[None, :] >= 0, 0, -8 * BIG)
    c[:, K_INV:K_INV + HALF] = np.float32(10000.0) ** (-np.arange(HALF, dtype=np.float32) / HALF)
    c[:, K_GRP:K_GRP + NE] = np.arange(NE) // (NE // NG)

    def onehot(dist, masked):
        n = np.maximum(dist, 0)
        ratio = np.log(np.maximum(n, 1).astype(np.float32) / np.float32(16)) / np.float32(np.log(8.0))
        large = 16 + (ratio.astype(np.float32) * np.float32(16)).astype(np.int32)
        b = np.where(n < 16, n, np.minimum(large, 31))
        o = np.zeros((33,) + dist.shape, np.float32)
        for i in range(32):
            o[i] = (b == i) & ~masked
        o[32] = masked
        return o

    x = (T - 1) - np.arange(OH_W)
    rev = onehot(x, x < 0)
    q = np.arange(P)[None, None, :] + P * np.arange(NT)[:, None, None]
    n = np.arange(16)[None, :, None]
    dc = q - (n * CMP + 31)
    oc = onehot(dc, (dc < 0) | (n >= NCMP)).reshape(33, -1)
    return c, np.concatenate([rev, oc], axis=1).astype(np.float32)


class Chain:

    def __init__(self, eng, sem):
        self.eng, self.sem, self.n = eng, sem, 0

    def __call__(self, ins):
        ins.then_inc(self.sem, 1)
        self.n += 1
        return self.n

    def sync(self, n=None):
        self.eng.wait_ge(self.sem, self.n if n is None else n)


def bc(ap, shape):
    while len(ap.shape) < len(shape):
        ap = ap.unsqueeze(len(ap.shape))
    return ap.broadcast_to(list(shape))


def build(nc, A, out):
    with ExitStack() as ctx:
        program(nc, A, out, ctx)


def program(nc, A, out, ctx):
    def sb(name, shape, dt=F32):
        return ctx.enter_context(nc.sbuf_tensor(name, shape, dt))

    def sem(name):
        return ctx.enter_context(nc.semaphore(name))

    bank = [ctx.enter_context(nc.psum_tensor(f"bank{i}", [P, 512], F32)) for i in range(8)]
    ring = sb("ring", [P, SLOTS, SLOT])
    x = sb("x_res", [P, NT, D])
    cst = sb("cst", [P, K_W])
    trig = sb("trig", [P, 2, NT, HALF])
    biasc = sb("biasc", [P, NT, H, 16])
    small = sb("small", [P, 700])
    AW = 24448
    arena = sb("arena", [P, AW])
    ident = cst[:, K_ID:K_ID + P]
    table = nc.dram_tensor("bias_table", [H, P, OH_W], F32, kind="Internal").ap()

    def region(at, *dims):
        n = int(np.prod(dims))
        assert at + n <= AW, (at, n)
        v = arena[:, at:at + n]
        if len(dims) == 2:
            v = v.rearrange("p (a b) -> p a b", b=dims[1])
        if len(dims) == 3:
            v = v.rearrange("p (a b c) -> p a b c", b=dims[1], c=dims[2])
        if len(dims) == 4:
            v = v.rearrange("p (a b c d) -> p a b c d", b=dims[1], c=dims[2], d=dims[3])
        return v

    def tiny(at, *dims):
        n = int(np.prod(dims))
        v = small[:, at:at + n]
        assert at + n <= 700
        if len(dims) == 2:
            v = v.rearrange("p (a b) -> p a b", b=dims[1])
        if len(dims) == 3:
            v = v.rearrange("p (a b c) -> p a b c", b=dims[1], c=dims[2])
        return v

    hT = region(0, KD, T)
    hA = region(2048, NT, D)
    mqT = region(2048, H, T)
    mixT = region(2048, KD, T)
    nqT = region(4096, 4, T)
    nkT = [region(5120, 2, T), region(22912, 2, T)]
    nv = region(5632, NT, 2, P)
    mp = region(6144, NT, M_W)
    fqT = region(7040, 4, T)
    fkT = region(8064, 4, T)
    fv = region(9088, NT, NQ)
    mkT = region(10112, H, T)
    mv = region(12160, NT, NQ)
    bias8 = region(13184, H, T)
    cqT = region(13184, 2, T)
    ckvT = region(13696, T)
    prob = region(15232, 2, 2, 384)
    probT = region(16768, 2, 2, 384)
    cw1v = region(15232, 16, HID)
    vcbd = region(17280, H, DH)
    pc = region(17792, NT, P)
    pcT = region(18048, NT, P)
    of_ = region(18304, NT, NQ)
    om_ = region(19328, NT, NQ)
    on_ = region(20352, NT, NQ)
    qtm = region(18304, NT, H * QK)
    uv = region(19840, NQ)
    oT = region(21376, 3, 4, T)
    cw1k = region(20352, 16, HID)
    kcp = region(23424, 2, 3, P)
    hvr = region(24192, P)
    stage_b = region(24192, P)
    stage_pe = region(24320, P)
    cmpt = region(17280, 5, 64)
    bias0 = region(21376, H, P)
    krt = region(17792, 4, NT * HALF)
    qrt = region(2048, 4, NT * H * HALF)
    mexp = region(15232, 4, T)
    mtmp = region(16768, 2, T)
    otmp = region(22400, 512)
    h2 = region(2048, NT, D)
    Ssel = region(4096, NT, NGRP + 1, P)
    STw = region(8448, NGRP + 1, T)
    Sw = region(12800, NT, NE, CAP)
    XT = region(14848, 2, KD, P)
    ysb = region(16896, 2, D)
    hid = region(18944, 3, F)
    hidT = region(19712, 2, P)
    accsb = region(19968, KD, T)
    ovw = region(4096, 3, SLOT)
    ovS = region(10240, NT, CAP)
    ovW = region(10368, NT, CAP)
    ovT = region(10496, T)
    wrt = region(22016, KD, NG + NE)
    g_att = tiny(0, KD)
    g_ffn = tiny(8, KD)
    g_q = tiny(16, 2)
    g_kv = tiny(18, 1)
    b1 = tiny(20, 2)
    nbm = tiny(22, 24)
    bf = tiny(46, H)
    w2k = tiny(54, 2, DH)
    w2v = tiny(182, DH)
    ss = tiny(246, 8)
    rstd = tiny(254, 8)
    rexp = tiny(680, 8)
    ng = tiny(270, NT, 24)
    mx = tiny(318, 64)
    sm = tiny(382, 64)
    coef = tiny(446, 64)
    hidc = tiny(510, 2, 32)
    kcT = tiny(574, 32)
    lf = tiny(606, NT, H)
    lft = tiny(622, 3, NT * H)
    rb = tiny(20, NG + NE)
    lg = tiny(56, NT, NG + NE)
    lgp = tiny(128, NT, 8)
    t8 = tiny(144, NT, 8)
    i8 = tiny(160, NT, 8)
    gf = tiny(176, 8)
    el = tiny(270, NT, NE)
    rw = tiny(334, 16)
    oh = tiny(350, 2, NE)
    Msel = tiny(414, NT, NE)
    Wsel = tiny(478, NT, NE)
    Rk = tiny(542, NT, NE)
    cnt = tiny(606, NE)
    cmax = tiny(640, 2)
    ovf = sb("ovf", [P, 1], I32)
    pos_i = sb("pos_i", [P, NT], I32)

    landed = [sem(f"landed{i}") for i in range(SLOTS)]
    s_mpb = sem("forget_cols_loaded")
    s_uk = sem("uk_loaded")
    stored = sem("stored")
    first = {}

    def csem(name):
        first[name] = sem(name)
        return first[name]

    s_small = csem("small_loaded")
    s_cw1 = csem("compress_w_loaded")
    s_cw2 = csem("compress_w2_loaded")
    s_uv = csem("uv_loaded")
    s_bias = csem("bias_loaded")
    s_prep = csem("loads_transposed")
    s_ss = csem("squares_summed")
    s_rstd = csem("rstd_ready")
    s_h = csem("h_ready")
    s_ht = csem("h_transposed_psum")
    s_hTd = csem("hT_by_vector")
    s_hTa = csem("hT_by_scalar")
    s_proj = csem("projected")
    s_evd = csem("projection_read_by_vector")
    s_eva = csem("projection_read_by_scalar")
    s_ach = csem("scalar_steps")
    s_dch = csem("vector_steps")
    s_gch = csem("gpsimd_steps")
    s_gc2 = csem("gpsimd_expert_steps")
    s_lss = csem("latent_squares")
    s_lrstd = csem("latent_rstd")
    s_lat = csem("latent_normed")
    s_latp = csem("latent_transposed_psum")
    s_latT = csem("latent_transposed")
    s_kr = csem("rope_key_stored")
    s_mk = csem("latent_key_psum")
    s_mke = csem("latent_key_read")
    s_mq = csem("latent_q_psum")
    s_mqe = csem("latent_q_read")
    s_qr = csem("latent_q_rotated")
    s_mqt = csem("latent_qT_psum")
    s_mqte = csem("latent_qT_read")
    s_mv = csem("latent_v_psum")
    s_mve = csem("latent_v_read")
    s_gx = csem("gate_logits_exp")
    s_z = csem("forget_logits_ready")
    s_ln = csem("forget_softplus")
    s_gz = csem("gelu_exp_wanted")
    s_gexp = csem("gelu_exp")
    s_sx = csem("cmp_exp_wanted")
    s_sexp = csem("cmp_exp")
    s_pz = csem("pe_block_zeroed")
    s_lf = csem("log_forget_ready")
    s_fb = csem("cum_forget_psum")
    s_fbe = csem("cum_forget_read")
    s_hc = csem("hidden_psum")
    s_hid = csem("hidden_ready")
    s_kv = csem("compressed_psum")
    s_kcT = csem("compressed_ready")
    s_sc = csem("cmp_scores_psum")
    s_pc = csem("cmp_probs_ready")
    s_pct = csem("cmp_probsT_psum")
    s_pcT = csem("cmp_probsT_ready")
    s_oc = csem("cmp_out_psum")
    s_oce = csem("cmp_out_read")
    s_qk = csem("scores_psum")
    s_max = csem("scores_shifted")
    s_exp = csem("probs_ready")
    s_pt = csem("probsT_psum")
    s_ptd = csem("probsT_by_vector")
    s_pta = csem("probsT_by_scalar")
    s_pv = csem("values_summed")
    s_oe = csem("branch_out_read")
    s_ot = csem("outT_psum")
    s_oTe = csem("outT_read_by_vector")
    s_oTa = csem("outT_read_by_scalar")
    s_mg = csem("merge_psum")
    s_mge = csem("merge_exp")
    s_mgd = csem("merge_read")
    s_op = csem("out_projected")
    s_ope = csem("out_added")
    s_wr = csem("router_w_loaded")
    s_lg = csem("logits_psum")
    s_rx = csem("router_exp_wanted")
    s_rxe = csem("router_exp")
    s_sel = csem("selected")
    s_rk = csem("ranks_psum")
    s_S = csem("selection_ready")
    s_sw = csem("weighted_selection")
    s_st = csem("selectionT_psum")
    s_std = csem("selectionT_read_by_vector")
    s_sta = csem("selectionT_read_by_scalar")
    s_yz = csem("zeros_ready")
    s_xg = csem("gathered_psum")
    s_xge = csem("gathered_read")
    s_gu = csem("gate_up_psum")
    s_ge = csem("gate_exp")
    s_hd = csem("expert_hidden")
    s_hdt = csem("expert_hiddenT_psum")
    s_hde = csem("expert_hiddenT_ready")
    s_y = csem("expert_out_psum")
    s_ye = csem("expert_out_read")
    s_dc2 = csem("vector_loop_steps")
    s_scat = csem("group_scattered")
    s_acc = csem("experts_summed")
    s_acd = csem("sum_read_by_vector")
    s_aca = csem("sum_read_by_scalar")
    s_fin = csem("sumT_psum")
    s_fine = csem("sum_added")
    s_ow = csem("overflow_w_loaded")
    s_o = [csem(f"overflow_{n}") for n in
           ("selected", "gathered", "gathered_read", "gate_up", "gate_exp", "hidden", "hiddenT",
            "hiddenT_read", "out", "out_read", "steps", "weightT", "weightT_read", "summed")]
    nums = [s.num for s in first.values()]
    assert nums == list(range(nums[0], nums[-1] + 1)), nums
    layer_sems = range(nums[0], nums[-1] + 1)
    ALL = [ENG.DVE, ENG.Activation, ENG.PE, ENG.Pool, ENG.SP]

    def w_in_cols(layer, c0, n):
        return A["w_in"][layer].rearrange("(p k) c -> p k c", k=KD)[:, :, c0:c0 + n]

    def slot_cols(n, w):
        return ring[:, n % SLOTS, 0:KD * w].rearrange("p (k c) -> p k c", k=KD)

    def attention_load(sp, layer, n):
        done = landed[n % SLOTS]

        def whole(src, w=256):
            sp.dma_start(slot_cols(n, w), src).then_inc(done, 16)

        if n == L_MPA:
            whole(w_in_cols(layer, C_G, 256))
        elif n == L_MPB:
            sp.dma_start(slot_cols(n, 192)[:, :, 0:184], w_in_cols(layer, C_G + 256, 184)).then_inc(done, 16)
            sp.dma_start(slot_cols(n, 192)[:, :, 184:192], w_in_cols(layer, C_FF, 8)).then_inc(s_mpb, 16)
        elif n in (L_NQ, L_NQ + 1):
            whole(w_in_cols(layer, C_NQ + 256 * (n - L_NQ), 256))
        elif n in (L_KC, L_KS, L_KW):
            whole(w_in_cols(layer, {L_KC: C_KC, L_KS: C_KS, L_KW: C_KW}[n], 256))
        elif n < L_UQ:
            b = {0: C_FQ, 1: C_FK, 2: C_FV}[(n - L_FQ) // 2]
            whole(w_in_cols(layer, b + 256 * ((n - L_FQ) % 2), 256))
        elif n == L_UQ:
            sp.dma_start(ring[:, n % SLOTS, 0:1536],
                         A["mla_w_uq"][layer].rearrange("(p j) c -> p (j c)", j=2)).then_inc(done, 16)
            sp.dma_start(ring[:, n % SLOTS, 1536:2048], A["mla_w_uk"][layer]).then_inc(s_uk, 16)
        elif n < L_OUT:
            half, i = divmod(n - L_MRG, 9)
            if 3 <= i < 6:
                w = A[("w_o_nsa", "w_o_mla", "w_o_fox")[i - 3]][layer].rearrange("(c p) n -> p c n", c=4)
                sp.dma_start(ring[:, n % SLOTS, :].rearrange("p (c n) -> p c n", c=4),
                             w[:, :, 512 * half:512 * half + 512]).then_inc(done, 16)
            else:
                q, b = i // 6, i % 3
                whole(w_in_cols(layer, C_MG + b * D + 512 * half + 256 * q, 256))
        else:
            i = n - L_OUT
            whole(A["w_out"][layer].rearrange("(k p) n -> p k n", k=KD)[:, :, 256 * i:256 * i + 256])

    def expert_load(sp, layer, e, i, slot, done):
        if i < 2:
            src = A["moe_w_gate" if i == 0 else "moe_w_up"][layer, e].rearrange("(p k) f -> p (k f)", k=KD)
        else:
            src = A["moe_w_down"][layer, e].rearrange("(p j) n -> p (j n)", j=2)
        sp.dma_start(slot, src).then_inc(done, 16)

    GROUP = [(e, m) for e in range(4) for m in (0, 1)] + [(e, 2) for e in range(4)]

    ohs = arena[0:33, 0:OH_W + NT * 16 * P]
    rbe = small[0:33, 0:H]
    tabs = region(11000, OH_W)[0:H]
    ang = region(8192, 6, NT * HALF)
    u_ld = sem("setup_loaded")
    u_ms = sem("setup_mask_row")
    u_pe = sem("setup_psum")
    u_cp = sem("setup_copied")
    u_tb = sem("table_stored")
    u_ch = sem("setup_steps")
    u_sn = sem("setup_angles")
    with nc.Block() as block:
        @block.sync
        def _(sp):
            sp.dma_start(x[:, :, :], A["x"][0].rearrange("(t p) d -> p t d", p=P)).then_inc(u_ld, 16)
            sp.dma_start(cst[:, :], A["shape_c"]).then_inc(u_ld, 16)
            for n in range(SLOTS):
                attention_load(sp, 0, n)

        @block.gpsimd
        def _(pool):
            pool.memset(small[32:33, 0:H], -BIG).then_inc(u_ms, 1)
            pool.wait_ge(u_ms, 1)
            pool.memset(rexp, -0.5)

        @block.tensor
        def _(pe):
            pe.wait_ge(u_ld, 96)
            pe.wait_ge(u_ms, 1)
            pe.matmul(bank[0][0:H, 0:OH_W], rbe, ohs[:, 0:OH_W], start=True, stop=True).then_inc(u_pe, 1)
            for t in range(NT):
                for n in range(16):
                    c = OH_W + (t * 16 + n) * P
                    last = pe.matmul(bank[1][:, (t * 16 + n) * H:(t * 16 + n + 1) * H], ohs[:, c:c + P], rbe,
                                     start=True, stop=True)
            last.then_inc(u_pe, 1)

        @block.scalar
        def _(act):
            act.dma_start(small[0:32, 0:H], A["rel_bias"]).then_inc(u_ld, 16)
            for t in range(NT):
                act.dma_start(pos_i[:, t:t + 1], A["positions"][0, t * P:(t + 1) * P].rearrange("(p o) -> p o", o=1))\
                   .then_inc(u_ld, 16)
            act.dma_start(ohs, A["shape_oh"]).then_inc(u_ld, 16)
            act.wait_ge(u_cp, 1)
            act.dma_start(table, tabs.unsqueeze(1).broadcast_to([H, P, OH_W])).then_inc(u_tb, 16)
            act.wait_ge(u_sn, 1)
            act.activation(trig[:, :, :, :], ang[:, 4:6, :].rearrange("p a (t i) -> p a t i", t=NT), ACT.Sin)

        @block.vector
        def _(dve):
            s = Chain(dve, u_ch)
            dve.wait_ge(u_ld, 96)
            dve.wait_ge(u_pe, 1)
            dve.tensor_scalar(tabs, bank[0][0:H, 0:OH_W], 8.0, None, ALU.mult).then_inc(u_cp, 1)
            s(dve.tensor_copy(small[:, 500:500 + NT], pos_i[:, :]))
            s.sync()
            for t in range(NT):
                s(dve.tensor_scalar(ang[:, 0, t * HALF:(t + 1) * HALF], cst[:, K_INV:K_INV + HALF],
                                    small[:, 500 + t:501 + t], None, ALU.mult))
            s.sync()
            MAGIC = float(1.5 * 2 ** 23)
            TWO_PI = 2 * np.pi
            HI, MID = 6.28125, 0.0019340515136718750
            LO = float(TWO_PI - HI - MID)
            for i, quarter in enumerate((0.25, 0.0)):
                s(dve.tensor_scalar(ang[:, 1, :], ang[:, 0, :], 1 / TWO_PI, quarter, ALU.mult, ALU.add))
                s.sync()
                s(dve.tensor_scalar(ang[:, 1, :], ang[:, 1, :], MAGIC, None, ALU.add))
                s.sync()
                s(dve.tensor_scalar(ang[:, 1, :], ang[:, 1, :], -MAGIC, None, ALU.add))
                s.sync()
                src = ang[:, 0, :]
                for part in (HI, MID, LO):
                    s(dve.scalar_tensor_tensor(out=ang[:, 2, :], in0=ang[:, 1, :], scalar=-part, in1=src,
                                               op0=ALU.mult, op1=ALU.add))
                    s.sync()
                    src = ang[:, 2, :]
                s(dve.tensor_scalar(ang[:, 2, :], ang[:, 2, :], quarter * TWO_PI, 3.1415925, ALU.add, ALU.min))
                s.sync()
                last = dve.tensor_scalar(ang[:, 4 + i, :], ang[:, 2, :], -3.1415925, None, ALU.max)
                if i == 0:
                    s(last)
                    s.sync()
            last.then_inc(u_sn, 1)
            dve.wait_ge(u_pe, 2)
            for t in range(NT):
                dve.tensor_scalar(biasc[:, t, :, :].rearrange("p h n -> p n h"),
                                  bank[1][:, 128 * t:128 * t + 128].rearrange("p (n h) -> p n h", h=H),
                                  8.0, None, ALU.mult)

    def norm_scalar(act):
        for t in range(NT):
            act.activation(hA[:, t, :], x[:, t, :], ACT.Square, accum_out=ss[:, t:t + 1]).then_inc(s_ss, 1)

    def picked(t):
        return Ssel[:, t, 0:NGRP, :].rearrange("p i (e c) -> p (i e) c", e=4)

    def norm_pool(pool, g, use):
        pool.wait_ge(s_ss, NT * (use + 1))
        g(pool.tensor_scalar(ss[:, 2:4], ss[:, 0:2], 1.0 / D, EPS, ALU.mult, ALU.add))
        g.sync()
        pool.tensor_tensor(rstd[:, 0:2], ss[:, 2:4], rexp[:, 0:2], ALU.pow).then_inc(s_rstd, 1)

    def norm_vector(dve, use):
        dve.wait_ge(s_rstd, use + 1)
        for t in range(NT):
            dve.tensor_scalar(hA[:, t, :], x[:, t, :], rstd[:, t:t + 1], None, ALU.mult).then_inc(s_h, 1)

    def norm_tensor(pe, use):
        pe.wait_ge(s_h, NT * (use + 1))
        for r in range(4):
            for j in range(2):
                for t in range(NT):
                    last = pe.transpose(bank[r][:, j * T + t * P:j * T + t * P + P],
                                        hA[:, t, 2 * r + j::KD], ident)
            last.then_inc(s_ht, 1)

    def norm_ready(pe, k, use):
        pe.wait_ge(s_hTa if (k // 2) % 2 else s_hTd, 2 * use + k // 4 + 1)

    def norm_read_vector(dve, gain, use):
        for r in (0, 2):
            dve.wait_ge(s_ht, 4 * use + r + 1)
            dve.tensor_tensor(hT[:, 2 * r:2 * r + 2, :], bank[r][:, :].rearrange("p (j t) -> p j t", j=2),
                              bc(gain[:, 2 * r:2 * r + 2], [P, 2, T]), ALU.mult).then_inc(s_hTd, 1)

    def norm_read_scalar(act, gain, use):
        for r in (1, 3):
            act.wait_ge(s_ht, 4 * use + r + 1)
            for j in range(2):
                last = act.activation(hT[:, 2 * r + j, :], bank[r][:, j * T:(j + 1) * T], ACT.Copy,
                                      scale=gain[:, 2 * r + j:2 * r + j + 1])
            last.then_inc(s_hTa, 1)

    JOBS = L_UQ
    UNITS = 16
    FOX, MLA, SLC, WIN = range(4)

    def jobs_read(pe, n):
        pe.wait_ge(s_eva if n % 2 else s_evd, n // 2 + 1)

    def score_cols(u, t, half):
        return (u // 2) * 8 + t * 4 + (u % 2) * 2 + half

    def seg(t):
        return (0, P) if t == 0 else (P, P + T)

    with nc.Fori(0, DEPTH) as layer:
        def ring_wait(eng, n):
            eng.wait_ge(landed[n % SLOTS], (layer * TURNS + (n // SLOTS + 1)) * 16)

        with nc.Block() as block:
            @block.sync
            def _(sp):
                for n in range(SLOTS, ATT_LOADS + SLOTS):
                    m = n - SLOTS
                    if m < L_UQ:
                        sp.wait_ge(s_proj, m + 1)
                    elif m == L_UQ:
                        sp.wait_ge(s_mq, 4)
                        sp.wait_ge(s_mk, 4)
                    elif m < L_OUT:
                        half, i = divmod(m - L_MRG, 9)
                        sp.wait_ge(s_mg, 12 * half + (4 if i < 3 else 10) + i % 3)
                    else:
                        sp.wait_ge(s_op, m - L_OUT + 1)
                    if n < ATT_LOADS:
                        attention_load(sp, layer, n)
                    else:
                        i = n - ATT_LOADS
                        expert_load(sp, layer, GROUP[i][0], GROUP[i][1], ring[:, n % SLOTS, :],
                                    landed[n % SLOTS])
                    if m == L_UQ:
                        sp.wait_ge(u_tb, 16)
                        sp.wait_ge(s_max, 4)
                        sp.dma_start(bias8, bass.AP(table.tensor, P - 1, [[OH_W - 1, P], [P * OH_W, H], [1, T]]))\
                          .then_inc(s_bias, 16)

            @block.gpsimd
            def _(pool):
                g = Chain(pool, s_gch)
                pool.memset(kcp[:, :, 2, :], 0.0).then_inc(s_pz, 1)
                pool.wait_ge(s_pz, 1)
                norm_pool(pool, g, 0)
                pool.wait_ge(s_rstd, 1)
                pool.wait_ge(s_lss, 4)
                g(pool.tensor_scalar(ss[:, 2:4], ss[:, 4:6], 1.0 / 256, EPS, ALU.mult, ALU.add))
                g.sync()
                g(pool.tensor_scalar(ss[:, 0:2], ss[:, 6:8], 1.0 / P, EPS, ALU.mult, ALU.add))
                g.sync()
                pool.tensor_tensor(rstd[:, 2:4], ss[:, 2:4], rexp[:, 0:2], ALU.pow).then_inc(s_lrstd, 1)
                pool.wait_ge(s_lrstd, 1)
                pool.tensor_tensor(rstd[:, 4:6], ss[:, 0:2], rexp[:, 0:2], ALU.pow).then_inc(s_lrstd, 1)

            @block.tensor
            def _(pe):
                norm_tensor(pe, 0)
                pe.wait_ge(s_small, 9 * 16)
                pe.transpose(bank[4][:, 0:24], stage_b[0:24, :], ident[0:24, 0:24])
                pe.transpose(bank[4][:, 32:48], stage_pe[0:16, :], ident[0:16, 0:16]).then_inc(s_prep, 1)

                def columns(dst, weight):
                    for k in range(KD):
                        last = pe.matmul(dst, weight(k), hT[:, k, :], start=(k == 0), stop=(k == KD - 1))
                    return last

                def rows(dst, t, weight):
                    for k in range(KD):
                        last = pe.matmul(dst, hT[:, k, t * P:(t + 1) * P], weight(k),
                                         start=(k == 0), stop=(k == KD - 1))
                    return last

                for n in range(JOBS):
                    ring_wait(pe, n)
                    if n == L_MPB:
                        pe.wait_ge(s_mpb, (layer + 1) * 16)
                    if n >= 4:
                        jobs_read(pe, n - 4)
                    b = bank[n % 4][:, :].rearrange("p (a c) -> p a c", a=2)
                    w = slot_cols(n, 192 if n == L_MPB else 256)
                    if n == 0:
                        for k in range(KD):
                            if k % 2 == 0:
                                norm_ready(pe, k, 0)
                            for a in range(2):
                                last = pe.matmul(b[:, a, :], hT[:, k, a * P:(a + 1) * P], w[:, k, :],
                                                 start=(k == 0 and a == 0), stop=(k == KD - 1), skip_group_check=True)
                        last.then_inc(s_proj, 1)
                        continue
                    for a in range(2):
                        if n in (L_NQ, L_NQ + 1, L_KC) or L_FQ <= n < L_FV:
                            last = columns(b[:, a, :], lambda k: w[:, k, a * P:(a + 1) * P])
                        elif n in (L_KS, L_KW):
                            if a == 0:
                                last = columns(b[:, 0, :], lambda k: w[:, k, 0:P])
                            else:
                                for t in range(NT):
                                    last = rows(b[:, 1, t * P:(t + 1) * P], t, lambda k: w[:, k, P:2 * P])
                        else:
                            wide = 192 if n == L_MPB else 256
                            last = rows(b[:, a, 0:wide], a, lambda k: w[:, k, 0:wide])
                    last.then_inc(s_proj, 1)

                pe.wait_ge(s_cw1, 32)
                pe.wait_ge(s_evd, L_KC // 2 + 1)
                for kv, w in enumerate((cw1k, cw1v)):
                    dst = bank[4][:, 64 * kv:64 * kv + 45].rearrange("p (g n) -> p g n", g=3)
                    for m in range(16):
                        last = pe.matmul(dst, w[:, m, :], kcp[:, kv, :, m:m + 8 * (NCMP - 1) + 1:8],
                                         start=(m == 0), stop=(m == 15))
                last.then_inc(s_hc, 1)
                pe.wait_ge(s_lat, 1)
                for j in range(2):
                    for t in range(NT):
                        pe.transpose(bank[5][:, (j * NT + t) * P:(j * NT + t + 1) * P],
                                     mp[:, t, M_CQ + j:M_CKV:2], ident)
                for t in range(NT):
                    pe.transpose(bank[6][:, t * P:(t + 1) * P], mp[:, t, M_CKV:M_KR], ident)
                for t in range(NT):
                    last = pe.transpose(bank[6][0:ROPE, T + t * P:T + (t + 1) * P], mp[:, t, M_KR:M_FF], ident)
                last.then_inc(s_latp, 1)
                pe.wait_ge(s_cw2, 48)
                pe.wait_ge(s_hid, 1)
                pe.matmul(bank[7][:, 0:32], w2k.rearrange("p a d -> p (a d)"), hidc[:, 0, :], start=True, stop=True)
                pe.matmul(bank[7][:, 64:128], hvr, w2v, start=True, stop=True).then_inc(s_kv, 1)
                ring_wait(pe, L_UQ)
                pe.wait_ge(s_uk, (layer + 1) * 16)
                pe.wait_ge(s_latT, 2)
                for n in range(JOBS - 4, JOBS):
                    jobs_read(pe, n)
                uq = ring[:, L_UQ % SLOTS, 0:1536].rearrange("p (j c) -> p j c", j=2)
                for i in range(4):
                    t, hf = divmod(i, 2)
                    for j in range(2):
                        last = pe.matmul(bank[i][:, 0:384], cqT[:, j, t * P:(t + 1) * P],
                                         uq[:, j, 384 * hf:384 * hf + 384], start=(j == 0), stop=(j == 1))
                    last.then_inc(s_mq, 1)
                pe.wait_ge(s_kr, 1)
                for i in range(4):
                    if i >= 2:
                        pe.wait_ge(s_mke, i - 1)
                    for a in range(2):
                        h = 2 * i + a
                        last = pe.matmul(bank[5 + i % 2][0:DH, a * T:(a + 1) * T],
                                         ring[:, L_UQ % SLOTS, 1536 + DH * h:1536 + DH * h + DH], ckvT,
                                         start=True, stop=True)
                    last.then_inc(s_mk, 1)
                pe.wait_ge(s_uv, 16)
                pe.wait_ge(s_kcT, 1)
                for t in range(NT):
                    pe.matmul(bank[(4, 7)[t]][:, :], ckvT[:, t * P:(t + 1) * P], uv, start=True, stop=True)\
                      .then_inc(s_mv, 1)
                pe.wait_ge(s_mke, 4)
                for t in range(NT):
                    for c in range(4):
                        for half in range(2):
                            r = slice(DH * half, DH * half + DH)
                            last = pe.matmul(bank[5 + half][:, (t * 4 + c) * 16:(t * 4 + c + 1) * 16],
                                             nqT[r, c, t * P:(t + 1) * P], kcT[r, 16 * (c // 2):16 * (c // 2) + 16],
                                             start=True, stop=True)
                last.then_inc(s_sc, 1)
                pe.wait_ge(s_qr, 1)
                for i in range(4):
                    for a in range(2):
                        h = 2 * i + a
                        for t in range(NT):
                            last = pe.transpose(bank[i][0:QK, (a * NT + t) * P:(a * NT + t + 1) * P],
                                                qtm[:, t, QK * h:QK * h + QK], ident)
                    last.then_inc(s_mqt, 1)
                pe.wait_ge(s_mve, 2)
                pe.wait_ge(s_lf, 1)
                for i in range(4):
                    if i >= 2:
                        pe.wait_ge(s_fbe, i - 1)
                    b = bank[(4, 7)[i % 2]]
                    for a in range(2):
                        h = 2 * i + a
                        pe.matmul(b[:, a * T:(a + 1) * T], lf[:, 0, h:h + 1].broadcast_to([P, P]),
                                  cst[:, K_TRI:K_TRI + T], start=True, stop=False, skip_group_check=True)
                        last = pe.matmul(b[:, a * T + P:(a + 1) * T], lf[:, 1, h:h + 1].broadcast_to([P, P]),
                                         cst[:, K_TRI:K_TRI + P], start=False, stop=True, skip_group_check=True)
                    last.then_inc(s_fb, 1)
                pe.wait_ge(s_pc, 1)
                for t in range(NT):
                    last = pe.transpose(bank[5][:, t * P:(t + 1) * P], pc[:, t, :], ident)
                last.then_inc(s_pct, 1)
                pe.wait_ge(s_pcT, 1)
                for t in range(NT):
                    pe.matmul(bank[6 - t][:, :], pcT[:, t, :], vcbd.rearrange("p h d -> p (h d)"),
                              start=True, stop=True).then_inc(s_oc, 1)

                def operands(u):
                    br, c = divmod(u, 4)
                    for half in range(2):
                        r = slice(DH * half, DH * half + DH)
                        h = 2 * c + half
                        if br == FOX:
                            yield half, fqT[r, c, :], fkT[r, c, :], [fv[:, t, DH * h:DH * h + DH] for t in range(NT)]
                        elif br == MLA:
                            yield half, mqT[0:QK, h, :], mkT[0:QK, h, :], [mv[:, t, DH * h:DH * h + DH] for t in range(NT)]
                        else:
                            g = slice(DH * (c // 2), DH * (c // 2) + DH)
                            yield half, nqT[r, c, :], nkT[br - SLC][r, c // 2, :], [nv[:, t, br - SLC, g] for t in range(NT)]

                def scores(u):
                    if u >= 2:
                        pe.wait_ge(s_max, u - 1)
                    for t in range(NT):
                        for half, q, k, _v in operands(u):
                            lo, hi = seg(t)
                            last = pe.matmul(bank[2 * (u % 2) + half][:, lo:hi], q[:, t * P:(t + 1) * P],
                                             k[:, 0:hi - lo], start=True, stop=True)
                    last.then_inc(s_qk, 1)

                def turn(u):
                    pe.wait_ge(s_exp, u + 1)
                    if u:
                        pe.wait_ge(s_ptd, u)
                        pe.wait_ge(s_pta, u)
                    for half in range(2):
                        for i in range(3):
                            last = pe.transpose(bank[4 + half][:, i * P:(i + 1) * P],
                                                prob[:, u % 2, half, i * P:(i + 1) * P], ident)
                        last.then_inc(s_pt, 1)

                def values(u):
                    pe.wait_ge(s_ptd, u + 1)
                    pe.wait_ge(s_pta, u + 1)
                    g = u // 2
                    if u % 2 == 0 and g >= 2:
                        pe.wait_ge(s_oe, g - 1)
                    o = bank[6 + g % 2][:, :].rearrange("p (t i d) -> p t i d", t=NT, i=4)
                    for half, _q, _k, v in operands(u):
                        i = (u % 2) * 2 + half
                        pt = probT[:, u % 2, half, :]
                        pe.matmul(o[:, 0, i, :], pt[:, 0:P], v[0], start=True, stop=True)
                        pe.matmul(o[:, 1, i, :], pt[:, P:2 * P], v[0], start=True, stop=False)
                        last = pe.matmul(o[:, 1, i, :], pt[:, 2 * P:3 * P], v[1], start=False, stop=True)
                    last.then_inc(s_pv, 1)

                pe.wait_ge(s_mqte, 4)
                pe.wait_ge(s_fbe, 4)
                pe.wait_ge(s_oce, 2)
                scores(0)
                scores(1)
                for u in range(UNITS):
                    if u + 2 < UNITS:
                        scores(u + 2)
                    turn(u)
                    if u >= 1:
                        values(u - 1)
                values(UNITS - 1)

                pe.wait_ge(s_oe, 8)
                for i in range(6):
                    src = (on_, om_, of_)[i // 2]
                    for a in range(2):
                        c = 2 * (i % 2) + a
                        for t in range(NT):
                            last = pe.transpose(bank[i][:, (a * NT + t) * P:(a * NT + t + 1) * P],
                                                src[:, t, c * P:(c + 1) * P], ident)
                    last.then_inc(s_ot, 1)
                pe.wait_ge(s_oTe, 3)
                pe.wait_ge(s_oTa, 3)
                for q in range(24):
                    m, b = divmod(q, 3)
                    half = m // 4
                    lo, lm = L_MRG + 9 * half + 3 + b, L_MRG + 9 * half + 6 * ((m // 2) % 2) + b
                    if m % 4 == 0:
                        ring_wait(pe, lo)
                    if m % 2 == 0:
                        ring_wait(pe, lm)
                    if q >= 4:
                        pe.wait_ge(s_mgd, q - 3)
                    wm = slot_cols(lm, 256)
                    wo = ring[:, lo % SLOTS, :].rearrange("p (c n) -> p c n", c=4)
                    columns(bank[q % 4][:, 0:T], lambda k: wm[:, k, (m % 2) * P:(m % 2 + 1) * P])
                    for c in range(4):
                        last = pe.matmul(bank[q % 4][:, T:2 * T], wo[:, c, (m % 4) * P:(m % 4 + 1) * P],
                                         oT[:, b, c, :], start=(c == 0), stop=(c == 3))
                    last.then_inc(s_mg, 1)
                pe.wait_ge(s_mgd, 24)
                for i in range(4):
                    ring_wait(pe, L_OUT + i)
                    w = slot_cols(L_OUT + i, 256)
                    for t in range(NT):
                        for k in range(KD):
                            last = pe.matmul(bank[4 + i][:, t * T:(t + 1) * T], mixT[:, k, t * P:(t + 1) * P],
                                             w[:, k, :], start=(k == 0), stop=(k == KD - 1))
                    last.then_inc(s_op, 1)

            @block.scalar
            def _(act):
                s = Chain(act, s_ach)
                norm_scalar(act)
                small_loads = [
                    (g_att, A["norm_attn"][layer].rearrange("(p k) -> p k", k=KD)),
                    (g_ffn, A["norm_ffn"][layer].rearrange("(p k) -> p k", k=KD)),
                    (g_q, A["mla_q_norm"][layer].rearrange("(p k) -> p k", k=2)),
                    (g_kv, A["mla_kv_norm"][layer].rearrange("(p k) -> p k", k=1)),
                    (b1[:, 0:1], A["cmp_k_b1"][layer].rearrange("(p k) -> p k", k=1)),
                    (b1[:, 1:2], A["cmp_v_b1"][layer].rearrange("(p k) -> p k", k=1)),
                    (bf, A["fox_b_f"][layer].partition_broadcast(P)),
                    (stage_b[0:24, :], A["b_merge"][layer].rearrange("(c p) -> c p", p=P)),
                    (stage_pe[0:16, :], A["cmp_pe"][layer].rearrange("(m a) d -> m (a d)", a=2)),
                ]
                for dst, src in small_loads:
                    act.dma_start(dst, src).then_inc(s_small, 16)
                act.dma_start(cw1k, A["cmp_k_w1"][layer].rearrange("(m p) h -> p m h", p=P), max_dma_last_dim=512).then_inc(s_cw1, 16)
                act.dma_start(cw1v, A["cmp_v_w1"][layer].rearrange("(m p) h -> p m h", p=P), max_dma_last_dim=512).then_inc(s_cw1, 16)
                for i in range(2):
                    act.dma_start(w2k[:, i, :], A["cmp_k_w2"][layer]).then_inc(s_cw2, 16)
                act.dma_start(w2v, A["cmp_v_w2"][layer]).then_inc(s_cw2, 16)
                act.dma_start(uv, A["mla_w_uv"][layer]).then_inc(s_uv, 16)
                act.wait_ge(s_small, 9 * 16)
                norm_read_scalar(act, g_att, 0)

                def read(n, dst, src):
                    act.wait_ge(s_proj, n + 1)
                    act.activation(dst, src, ACT.Copy).then_inc(s_eva, 1)

                two = lambda b: b[:, :].rearrange("p (a c) -> p a c", a=2)
                read(1, mp[:, :, 256:448], two(bank[1])[:, :, 0:192])
                act.wait_ge(s_evd, 1)
                act.wait_ge(s_eva, 1)
                for t in range(NT):
                    act.activation(of_[:, t, 0:256], mp[:, t, M_CQ:M_CKV], ACT.Square,
                                   accum_out=ss[:, 4 + t:5 + t]).then_inc(s_lss, 1)
                    act.activation(of_[:, t, 256:384], mp[:, t, M_CKV:M_KR], ACT.Square,
                                   accum_out=ss[:, 6 + t:7 + t]).then_inc(s_lss, 1)
                read(3, nqT[:, 2:4, :], two(bank[3]))
                act.activation(ng, mp[:, :, 0:24], ACT.Exp, scale=-1.0).then_inc(s_gx, 1)
                act.wait_ge(s_z, 1)
                s(act.activation(lft[:, 2, :], lft[:, 1, :], ACT.Exp, scale=-1.0))
                s.sync()
                act.activation(lft[:, 1, :], lft[:, 2, :], ACT.Ln, bias=1.0).then_inc(s_ln, 1)
                act.wait_ge(s_proj, L_KS + 1)
                for g in range(2):
                    for half in range(2):
                        act.activation(nkT[0][DH * half:DH * half + DH, g, :], bank[1][DH * g:DH * g + DH, 0:T], ACT.Copy)
                act.activation(nv[:, :, 0, :], two(bank[1])[:, 1, :].rearrange("p (t d) -> p t d", t=NT), ACT.Copy)\
                   .then_inc(s_eva, 1)
                read(7, fqT[:, 0:2, :], two(bank[3]))
                read(9, fkT[:, 0:2, :], two(bank[1]))
                read(11, fv[:, :, 0:256], two(bank[3]))
                act.wait_ge(s_gz, 1)
                act.activation(cmpt[:, 2, :], cmpt[:, 1, :], ACT.Exp, scale=-2 * 0.7978845608028654)\
                   .then_inc(s_gexp, 1)
                act.wait_ge(s_latp, 1)
                act.wait_ge(s_latT, 2)
                act.wait_ge(u_tb, 16)
                act.activation(mkT[DH:QK, :, :], bank[6][0:ROPE, T:2 * T].unsqueeze(1).broadcast_to([ROPE, H, T]),
                               ACT.Copy).then_inc(s_kr, 1)
                for i in range(4):
                    act.wait_ge(s_mk, i + 1)
                    act.activation(mkT[0:DH, 2 * i:2 * i + 2, :],
                                   bank[5 + i % 2][0:DH, :].rearrange("p (a t) -> p a t", a=2), ACT.Copy)\
                       .then_inc(s_mke, 1)
                for t in range(NT):
                    act.wait_ge(s_mv, t + 1)
                    act.activation(mv[:, t, :], bank[(4, 7)[t]][:, :], ACT.Copy).then_inc(s_mve, 1)
                act.wait_ge(s_sx, 1)
                act.activation(pc, pc, ACT.Exp, scale=0.125).then_inc(s_sexp, 1)
                for i in range(4):
                    act.wait_ge(s_mqt, i + 1)
                    act.activation(mqT[0:QK, 2 * i:2 * i + 2, :],
                                   bank[i][0:QK, :].rearrange("p (a t) -> p a t", a=2), ACT.Copy)\
                       .then_inc(s_mqte, 1)
                for u in range(UNITS + 1):
                    if u < UNITS:
                        scale = QK ** -0.5 if u // 4 == MLA else DH ** -0.5
                        act.wait_ge(s_max, u + 1)
                        for half in range(2):
                            for t in range(NT):
                                lo, hi = seg(t)
                                c = score_cols(u, t, half)
                                pr = prob[:, u % 2, half, lo:hi]
                                last = act.activation(pr, pr, ACT.Exp, scale=scale, bias=mx[:, c:c + 1],
                                                      accum_out=sm[:, c:c + 1])
                        last.then_inc(s_exp, 1)
                    if u >= 1:
                        act.wait_ge(s_pt, 2 * u)
                        if u >= 3:
                            act.wait_ge(s_pv, u - 2)
                        act.activation(probT[:, (u - 1) % 2, 1, :], bank[5][:, 0:384], ACT.Copy)\
                           .then_inc(s_pta, 1)
                for i in (1, 3, 5):
                    act.wait_ge(s_ot, i + 1)
                    act.activation(oT[:, i // 2, 2:4, :], two(bank[i]), ACT.Copy).then_inc(s_oTa, 1)
                for q in range(24):
                    m, b = divmod(q, 3)
                    act.wait_ge(s_mg, q + 1)
                    if q >= 4:
                        act.wait_ge(s_mgd, q - 3)
                    act.activation(mexp[:, q % 4, :], bank[q % 4][:, 0:T], ACT.Exp, scale=-1.0,
                                   bias=nbm[:, b * KD + m:b * KD + m + 1]).then_inc(s_mge, 1)

            @block.vector
            def _(dve):
                s = Chain(dve, s_dch)
                two = lambda b: b[:, :].rearrange("p (a c) -> p a c", a=2)
                norm_vector(dve, 0)
                dve.wait_ge(s_small, 9 * 16)
                norm_read_vector(dve, g_att, 0)
                dve.wait_ge(s_prep, 1)
                dve.wait_ge(s_pz, 1)
                dve.tensor_scalar(nbm, bank[4][:, 0:24], -1.0, None, ALU.mult)
                for kv in range(2):
                    last = dve.tensor_copy(kcp[:, kv, 2, 0:16], bank[4][:, 32:48])
                s(last)

                def read(n, dst, src):
                    dve.wait_ge(s_proj, n + 1)
                    dve.tensor_copy(dst, src).then_inc(s_evd, 1)

                read(0, mp[:, :, 0:256], two(bank[0]))
                read(2, nqT[:, 0:2, :], two(bank[2]))
                dve.wait_ge(s_eva, 1)
                z = lft[:, 0, :].rearrange("p (t h) -> p t h", t=NT)
                s(dve.tensor_tensor(z, mp[:, :, M_FF:M_W], bf.unsqueeze(1).broadcast_to([P, NT, H]), ALU.add))
                s.sync()
                s(dve.tensor_scalar(lft[:, 2, :], lft[:, 0, :], -1.0, None, ALU.mult))
                s.sync()
                dve.tensor_tensor(lft[:, 1, :], lft[:, 0, :], lft[:, 2, :], ALU.max).then_inc(s_z, 1)
                dve.wait_ge(s_lrstd, 2)
                for t in range(NT):
                    s(dve.tensor_scalar(mp[:, t, M_CQ:M_CKV], mp[:, t, M_CQ:M_CKV], rstd[:, 2 + t:3 + t], None, ALU.mult))
                    s(dve.tensor_scalar(mp[:, t, M_CKV:M_KR], mp[:, t, M_CKV:M_KR], rstd[:, 4 + t:5 + t], None, ALU.mult))
                k1, k2 = mp[:, :, M_KR:M_KR + HALF], mp[:, :, M_KR + HALF:M_FF]
                cos, sin = trig[:, 0], trig[:, 1]
                prod = [krt[:, i, :].rearrange("p (t c) -> p t c", t=NT) for i in range(4)]
                for i, (a, b) in enumerate(((k1, cos), (k2, sin), (k1, sin), (k2, cos))):
                    s(dve.tensor_tensor(prod[i], a, b, ALU.mult))
                s.sync()
                s(dve.tensor_tensor(k1, prod[0], prod[1], ALU.subtract))
                dve.tensor_tensor(k2, prod[2], prod[3], ALU.add).then_inc(s_lat, 1)
                dve.wait_ge(s_proj, L_KC + 1)
                for par in range(2):
                    for g in range(2):
                        last = dve.tensor_copy(kcp[DH * par:DH * par + DH, :, g, :],
                                               two(bank[L_KC % 4])[DH * g:DH * g + DH, :, par::2])
                last.then_inc(s_evd, 1)
                dve.wait_ge(s_gx, 1)
                s(dve.tensor_scalar(ng, ng, 1.0, None, ALU.add))
                s.sync()
                s(dve.reciprocal(ng, ng))
                dve.wait_ge(s_ln, 1)
                lf2 = lf.rearrange("p t h -> p (t h)")
                s(dve.tensor_scalar(lft[:, 2, :], lft[:, 0, :], 0.0, None, ALU.min))
                s.sync()
                dve.tensor_tensor(lf2, lft[:, 2, :], lft[:, 1, :], ALU.subtract).then_inc(s_lf, 1)
                dve.wait_ge(s_proj, L_KW + 1)
                for g in range(2):
                    for half in range(2):
                        dve.tensor_copy(nkT[1][DH * half:DH * half + DH, g, :], bank[2][DH * g:DH * g + DH, 0:T])
                dve.tensor_copy(nv[:, :, 1, :], two(bank[2])[:, 1, :].rearrange("p (t d) -> p t d", t=NT))\
                   .then_inc(s_evd, 1)
                read(8, fqT[:, 2:4, :], two(bank[0]))
                read(10, fkT[:, 2:4, :], two(bank[2]))
                read(12, fv[:, :, 256:512], two(bank[0]))
                Z, Q, E = cmpt[:, 0, :], cmpt[:, 1, :], cmpt[:, 2, :]
                Zb = Z.rearrange("p (v g n) -> p v g n", v=2, g=2)
                s(dve.memset(Z, 0.0))
                dve.wait_ge(s_hc, 1)
                for kv in range(2):
                    s(dve.tensor_tensor(cmpt[:, 3, kv:kv + 1], bank[4][:, 64 * kv + 30:64 * kv + 31],
                                        b1[:, kv:kv + 1], ALU.add))
                s.sync()
                for kv in range(2):
                    s(dve.tensor_scalar(Zb[:, kv, :, 0:NCMP],
                                        bank[4][:, 64 * kv:64 * kv + 30].rearrange("p (g n) -> p g n", g=2),
                                        cmpt[:, 3, kv:kv + 1], None, ALU.add))
                s.sync()
                s(dve.tensor_tensor(Q, Z, Z, ALU.mult))
                s.sync()
                s(dve.tensor_scalar(Q, Q, 0.044715, 1.0, ALU.mult, ALU.add))
                s.sync()
                dve.tensor_tensor(Q, Q, Z, ALU.mult).then_inc(s_gz, 1)
                dve.wait_ge(s_latp, 1)
                dve.tensor_tensor(cqT, two(bank[5]), bc(g_q, [P, 2, T]), ALU.mult).then_inc(s_latT, 1)
                dve.tensor_scalar(ckvT, bank[6][:, 0:T], g_kv, None, ALU.mult).then_inc(s_latT, 1)
                dve.wait_ge(s_gexp, 1)
                s(dve.tensor_scalar(E, E, 1.0, None, ALU.add))
                s.sync()
                s(dve.reciprocal(E, E))
                s.sync()
                s(dve.tensor_tensor(hidc.rearrange("p a b -> p (a b)"), Z, E, ALU.mult))
                s.sync()
                for g in range(2):
                    last = dve.tensor_copy(hvr[:, 64 * g:64 * g + 64].rearrange("p (a n) -> p a n", a=4),
                                           hidc[:, 1, 16 * g:16 * g + 16].unsqueeze(1).broadcast_to([P, 4, 16]))
                last.then_inc(s_hid, 1)
                dve.wait_ge(s_kv, 1)
                dve.tensor_copy(kcT, bank[7][:, 0:32])
                dve.tensor_tensor(vcbd, bank[7][:, 64:128].unsqueeze(1).broadcast_to([P, H, DH]),
                                  bc(cst[:, K_HM:K_HM + H], [P, H, DH]), ALU.mult).then_inc(s_kcT, 1)
                for i in range(4):
                    t, hf = divmod(i, 2)
                    dve.wait_ge(s_mq, i + 1)
                    s(dve.tensor_copy(qtm[:, t, 384 * hf:384 * hf + 384], bank[i][:, 0:384]))
                s.sync()
                qv = qtm.rearrange("p t (h d) -> p t h d", h=H)
                prod = [qrt[:, i, :].rearrange("p (t h c) -> p t h c", t=NT, h=H) for i in range(4)]
                for i, (lo, tr) in enumerate(((DH, 0), (DH + HALF, 1), (DH, 1), (DH + HALF, 0))):
                    for t in range(NT):
                        s(dve.tensor_tensor(prod[i][:, t], qv[:, t, :, lo:lo + HALF],
                                            trig[:, tr, t, :].unsqueeze(1).broadcast_to([P, H, HALF]), ALU.mult))
                s.sync()
                for t in range(NT):
                    s(dve.tensor_tensor(qv[:, t, :, DH:DH + HALF], prod[0][:, t], prod[1][:, t], ALU.subtract))
                    last = dve.tensor_tensor(qv[:, t, :, DH + HALF:QK], prod[2][:, t], prod[3][:, t], ALU.add)
                    if t == 0:
                        s(last)
                last.then_inc(s_qr, 1)
                dve.wait_ge(s_sc, 1)
                pcv = pc.rearrange("p t (c s n) -> p (t c) s n", s=2, n=16)
                bcv = biasc[:, :, :, :].rearrange("p t (c s) n -> p (t c) s n", s=2)
                for half in range(2):
                    s(dve.tensor_tensor(pcv[:, :, half, :], bank[5 + half][:, 0:128].rearrange("p (a n) -> p a n", n=16),
                                        bcv[:, :, half, :], ALU.add))
                s.sync()
                pch = pc.rearrange("p t (h n) -> p (t h) n", n=16)
                cm, cs = coef[:, 0:16], coef[:, 16:32]
                s(dve.tensor_reduce(cm, pch, AX.X, ALU.max))
                s.sync()
                dve.tensor_tensor(pch, pch, bc(cm, [P, 16, 16]), ALU.subtract).then_inc(s_sx, 1)
                dve.wait_ge(s_sexp, 1)
                s(dve.tensor_reduce(cs, pch, AX.X, ALU.add))
                s.sync()
                s(dve.reciprocal(cs, cs))
                s.sync()
                gates = ng.rearrange("p t (c s b) -> p t c s b", s=2, c=4)
                for t in range(NT):
                    s(dve.tensor_tensor(cs[:, 8 * t:8 * t + 8].rearrange("p (c s) -> p c s", s=2),
                                        cs[:, 8 * t:8 * t + 8].rearrange("p (c s) -> p c s", s=2),
                                        gates[:, t, :, :, 0], ALU.mult))
                    s(dve.tensor_tensor(pc[:, t, :].rearrange("p (h n) -> p h n", n=16),
                                        pc[:, t, :].rearrange("p (h n) -> p h n", n=16),
                                        cst[:, K_OK + 16 * t:K_OK + 16 * t + 16].unsqueeze(1).broadcast_to([P, H, 16]),
                                        ALU.mult))
                s.sync()
                dve.tensor_tensor(pch, pch, bc(cs, [P, 16, 16]), ALU.mult).then_inc(s_pc, 1)
                for i in range(4):
                    dve.wait_ge(s_fb, i + 1)
                    b = two(bank[(4, 7)[i % 2]])
                    mask = cst[:, K_MASK:K_MASK + T].unsqueeze(1).broadcast_to([P, 2, T])
                    dve.scalar_tensor_tensor(out=bias8[:, 2 * i:2 * i + 2, :], in0=b, scalar=-8.0, in1=mask,
                                             op0=ALU.mult, op1=ALU.add)
                    dve.scalar_tensor_tensor(out=bias0[:, 2 * i:2 * i + 2, :], in0=b[:, :, 0:P], scalar=-8.0,
                                             in1=mask[:, :, P:T], op0=ALU.mult, op1=ALU.add).then_inc(s_fbe, 1)
                dve.wait_ge(s_pct, 1)
                dve.tensor_copy(pcT.rearrange("p t q -> p (t q)"), bank[5][:, 0:T]).then_inc(s_pcT, 1)
                for t in range(NT):
                    dve.wait_ge(s_oc, t + 1)
                    last = dve.tensor_copy(on_[:, t, :], bank[6 - t][:, :])
                    last.then_inc(s_oce, 1)
                dve.wait_ge(s_oce, 2)

                def shifted(u):
                    br, c = divmod(u, 4)
                    dve.wait_ge(s_qk, u + 1)
                    if u == 0:
                        dve.wait_ge(s_fbe, 4)
                    if u == 4 * SLC:
                        dve.wait_ge(s_bias, 16)
                    if u >= 2:
                        dve.wait_ge(s_pt, 2 * u - 2)
                    for half in range(2):
                        h = 2 * c + half
                        for t in range(NT):
                            lo, hi = seg(t)
                            if br == MLA:
                                b = cst[:, K_MASK + P * (1 - t):K_MASK + T]
                            elif t == 1:
                                b = bias8[:, h, :]
                            else:
                                b = bias0[:, h, :] if br == FOX else bias8[:, h, P:T]
                            col = score_cols(u, t, half)
                            last = dve.tensor_tensor_reduce(
                                out=prob[:, u % 2, half, lo:hi], in0=bank[2 * (u % 2) + half][:, lo:hi], in1=b,
                                scale=1.0, scalar=-3e38, op0=ALU.add, op1=ALU.max, accum_out=mx[:, col:col + 1])
                            s(last)
                    s.sync()
                    m = mx[:, 8 * (u // 2):8 * (u // 2) + 8].rearrange("p (t v s) -> p t v s", t=NT, s=2)[:, :, u % 2, :]
                    scale = QK ** -0.5 if br == MLA else DH ** -0.5
                    dve.tensor_scalar(m, m, -scale, None, ALU.mult).then_inc(s_max, 1)

                def read_out(g):
                    br, gg = divmod(g, 2)
                    dve.wait_ge(s_pv, 2 * g + 2)
                    r = coef[:, 8 * g:8 * g + 8]
                    s(dve.reciprocal(r, sm[:, 8 * g:8 * g + 8]))
                    s.sync()
                    if br >= SLC:
                        for t in range(NT):
                            rt = r[:, 4 * t:4 * t + 4].rearrange("p (c s) -> p c s", s=2)
                            s(dve.tensor_tensor(rt, rt, gates[:, t, 2 * gg:2 * gg + 2, :, br - SLC + 1], ALU.mult))
                        s.sync()
                    o = bank[6 + g % 2][:, :].rearrange("p (a d) -> p a d", d=DH)
                    acc = (of_, om_, on_, on_)[br][:, :, 256 * gg:256 * gg + 256]
                    if br < SLC:
                        dst = acc.rearrange("p t (i d) -> p t i d", d=DH)
                        for t in range(NT):
                            last = dve.tensor_tensor(dst[:, t], o[:, 4 * t:4 * t + 4, :],
                                                     bc(r[:, 4 * t:4 * t + 4], [P, 4, DH]), ALU.mult)
                        last.then_inc(s_oe, 1)
                    else:
                        s(dve.tensor_tensor(otmp.rearrange("p (a d) -> p a d", d=DH), o, bc(r, [P, 8, DH]), ALU.mult))
                        s.sync()
                        dve.tensor_tensor(acc, acc, otmp.rearrange("p (t c) -> p t c", t=NT), ALU.add)\
                           .then_inc(s_oe, 1)
                        dve.wait_ge(s_oe, g + 1)

                for u in range(UNITS + 2):
                    if u < UNITS:
                        shifted(u)
                    if 1 <= u <= UNITS:
                        dve.wait_ge(s_pt, 2 * u - 1)
                        if u >= 3:
                            dve.wait_ge(s_pv, u - 2)
                        dve.tensor_copy(probT[:, (u - 1) % 2, 0, :], bank[4][:, 0:384]).then_inc(s_ptd, 1)
                    if u >= 3 and u % 2 == 1:
                        read_out((u - 3) // 2)
                for i in (0, 2, 4):
                    dve.wait_ge(s_ot, i + 1)
                    dve.tensor_copy(oT[:, i // 2, 0:2, :], two(bank[i])).then_inc(s_oTe, 1)
                for q in range(24):
                    m, b = divmod(q, 3)
                    e = mexp[:, q % 4, :]
                    dve.wait_ge(s_mge, q + 1)
                    s(dve.tensor_scalar(e, e, 1.0, None, ALU.add))
                    s.sync()
                    s(dve.reciprocal(e, e))
                    s.sync()
                    if b == 0:
                        dve.tensor_tensor(mixT[:, m, :], e, bank[q % 4][:, T:2 * T], ALU.mult).then_inc(s_mgd, 1)
                    else:
                        s(dve.tensor_tensor(mtmp[:, q % 2, :], e, bank[q % 4][:, T:2 * T], ALU.mult))
                        s.sync()
                        dve.wait_ge(s_mgd, q)
                        dve.tensor_tensor(mixT[:, m, :], mixT[:, m, :], mtmp[:, q % 2, :], ALU.add).then_inc(s_mgd, 1)
                for i in range(4):
                    dve.wait_ge(s_op, i + 1)
                    xi = x[:, :, 256 * i:256 * i + 256]
                    dve.tensor_tensor(xi, xi, two(bank[4 + i]), ALU.add)

        with nc.Block() as block:
            def got(eng, j, slot):
                eng.wait_ge(landed[slot], (layer * TURNS + j + (ATT_LOADS // SLOTS + 1)) * 16)

            @block.sync
            def _(sp):
                sp.dma_start(wrt[:, :, 0:NG], A["moe_w_grp"][layer].rearrange("(p k) g -> p k g", k=KD)).then_inc(s_wr, 16)
                sp.dma_start(wrt[:, :, NG:], A["moe_w_router"][layer].rearrange("(p k) g -> p k g", k=KD)).then_inc(s_wr, 16)
                sp.dma_start(rb[:, 0:NG], A["moe_b_grp"][layer].partition_broadcast(P)).then_inc(s_wr, 16)
                sp.dma_start(rb[:, NG:], A["moe_b_router"][layer].partition_broadcast(P)).then_inc(s_wr, 16)
                with sp.Fori(0, NGRP - 1) as j:
                    for i, (e, m) in enumerate(GROUP):
                        if i == 0:
                            sp.wait_ge(s_gu, j + 1)
                        if i == 8:
                            sp.wait_ge(s_y, j * 2 + 2)
                        expert_load(sp, layer, j * 4 + (4 + e), m, ring[:, i, :], landed[i])
                with sp.If(layer < DEPTH - 1):
                    for n in range(SLOTS):
                        if n == 0:
                            sp.wait_ge(s_gu, NGRP)
                        if n == 8:
                            sp.wait_ge(s_y, 2 * NGRP)
                        attention_load(sp, DEPTH - 1, n)

            @block.gpsimd
            def _(pool):
                g = Chain(pool, s_gc2)
                norm_pool(pool, g, 1)
                pool.wait_ge(s_rstd, 2)
                g(pool.memset(Ssel[:, :, NGRP, :], 0.0))
                g.sync()
                g(pool.memset(STw[:, 0, :], 0.0))
                g.sync()
                pool.memset(ysb, 0.0).then_inc(s_yz, 1)
                for t in range(NT):
                    pool.wait_ge(s_S, t + 1)
                    pool.tensor_tensor(Sw[:, t], picked(t), bc(Wsel[:, t, :], [P, NE, CAP]), ALU.mult).then_inc(s_sw, 1)

            @block.tensor
            def _(pe):
                pe.wait_ge(s_yz, 1)
                norm_tensor(pe, 1)
                pe.wait_ge(s_wr, 64)
                for k in range(KD):
                    if k % 2 == 0:
                        norm_ready(pe, k, 1)
                    for t in range(NT):
                        last = pe.matmul(bank[4][:, t * 64:t * 64 + NG + NE], hT[:, k, t * P:(t + 1) * P], wrt[:, k, :],
                                         start=(k == 0 and t == 0), stop=(k == KD - 1), skip_group_check=True)
                last.then_inc(s_lg, 1)
                zeros = ysb[:, 0, :].bitcast(mybir.dt.bfloat16)
                for b in range(4):
                    pe.matmul(bank[b][:, :], zeros[:, 0:P], zeros[:, 0:512], start=True, stop=False,
                              skip_group_check=True)
                pe.wait_ge(s_sel, 1)
                strict, ones = cst[:, K_STRICT:K_STRICT + P], cst[:, K_ONES:K_ONES + P]
                pe.matmul(bank[5][:, 0:NE], strict, Msel[:, 0, :], start=True, stop=True)
                pe.matmul(bank[5][:, NE:2 * NE], ones, Msel[:, 0, :], start=True, stop=False)
                pe.matmul(bank[5][:, NE:2 * NE], strict, Msel[:, 1, :], start=False, stop=True)
                pe.matmul(bank[5][:, 2 * NE:3 * NE], ones, Msel[:, 0, :], start=True, stop=False)
                pe.matmul(bank[5][:, 2 * NE:3 * NE], ones, Msel[:, 1, :], start=False, stop=True).then_inc(s_rk, 1)

                def gather(sel):
                    for half in range(2):
                        b = bank[7 - half]
                        for a in range(4):
                            for t in range(NT):
                                last = pe.matmul(b[:, a * P:(a + 1) * P], h2[:, t, 4 * half + a::KD], sel(t),
                                                 start=(t == 0), stop=(t == NT - 1))
                        last.then_inc(s_xg, 1)

                pe.wait_ge(s_S, 2)
                gather(lambda t: Ssel[:, t, 0, :])
                for i in range(4):
                    t, r = divmod(i, 2)
                    pe.wait_ge(s_sw, t + 1)
                    if i >= 2:
                        pe.wait_ge(s_std if i % 2 == 0 else s_sta, (i - 2) // 2 + 1)
                    for a in range(4):
                        last = pe.transpose(bank[4 + i % 2][:, a * P:(a + 1) * P],
                                            Sw[:, t, 4 * (4 * r + a):4 * (4 * r + a) + 4, :].rearrange("p e c -> p (e c)"),
                                            ident)
                    last.then_inc(s_st, 1)
                pe.wait_ge(s_std, 2)
                pe.wait_ge(s_sta, 2)

                def scatter(q, rhs):
                    for m in range(KD):
                        last = pe.matmul(bank[m // 2][:, (m % 2) * T:(m % 2 + 1) * T], ysb[:, q, m * P:(m + 1) * P], rhs,
                                         start=False, stop=False, skip_group_check=True)
                    return last

                with pe.Fori(0, NGRP // 2) as j:
                    for q in range(2):
                        pe.wait_ge(s_xge, j * 4 + (2 * q + 2))
                        pe.wait_ge(s_hde, j * 2 + q)
                        for i in range(8):
                            got(pe, j * 2 + q, i)
                        for k in range(KD):
                            for e in range(4):
                                w = ring[:, 2 * e:2 * e + 2, k * F:(k + 1) * F]
                                last = pe.matmul(bank[4][CAP * e:CAP * e + CAP, :].rearrange("p (a f) -> p a f", a=2),
                                                 XT[:, q, k, CAP * e:CAP * e + CAP], w,
                                                 start=(k == 0), stop=(k == KD - 1))
                        last.then_inc(s_gu, 1)
                        pe.wait_ge(s_ye, j * 4 + 2 * q)
                        gather(lambda t: Ssel[:, t, j * 2 + (q + 1), :])
                        pe.wait_ge(s_hd, j * 2 + (q + 1))
                        for a in range(2):
                            last = pe.transpose(bank[4][:, a * P:(a + 1) * P], hid[:, 2, a::2], ident)
                        last.then_inc(s_hdt, 1)
                        scatter(1 - q, STw[:, j * 2 + q, :]).then_inc(s_scat, 1)
                        pe.wait_ge(s_hde, j * 2 + (q + 1))
                        pe.wait_ge(s_xge, j * 4 + (2 * q + 4))
                        for i in range(8, 12):
                            got(pe, j * 2 + q, i)
                        for n in range(2):
                            for a in range(2):
                                for e in range(4):
                                    last = pe.matmul(bank[5 + n][CAP * e:CAP * e + CAP, :],
                                                     hidT[:, a, CAP * e:CAP * e + CAP],
                                                     ring[:, 8 + e, a * D + 512 * n:a * D + 512 * n + 512],
                                                     start=(a == 0), stop=(a == 1))
                            last.then_inc(s_y, 1)
                pe.wait_ge(s_ye, 2 * NGRP)
                scatter(1, STw[:, NGRP, :]).then_inc(s_acc, 1)
                pe.wait_ge(s_acd, 2)
                pe.wait_ge(s_aca, 2)
                for t in range(NT):
                    for r in range(2):
                        for a in range(4):
                            last = pe.transpose(bank[4 + 2 * t + r][:, a * P:(a + 1) * P],
                                                accsb[:, 4 * r + a, t * P:(t + 1) * P], ident)
                        last.then_inc(s_fin, 1)

            @block.scalar
            def _(act):
                norm_scalar(act)
                norm_read_scalar(act, g_ffn, 1)
                act.wait_ge(s_rx, 1)
                act.activation(lgp[:, :, 0:NG], lgp[:, :, 0:NG], ACT.Exp).then_inc(s_rxe, 1)
                act.wait_ge(s_rx, 2)
                act.activation(rw[:, 4:6], rw[:, 2:4], ACT.Exp).then_inc(s_rxe, 1)
                for i in (1, 3):
                    t, r = divmod(i, 2)
                    act.wait_ge(s_st, i + 1)
                    act.activation(STw[:, 1 + 4 * r:5 + 4 * r, t * P:(t + 1) * P],
                                   bank[5][:, :].rearrange("p (a c) -> p a c", a=4), ACT.Copy).then_inc(s_sta, 1)
                act.wait_ge(s_yz, 1)
                with act.Fori(0, NGRP // 2) as j:
                    for q in range(2):
                        act.wait_ge(s_gu, j * 2 + (q + 1))
                        act.wait_ge(s_hd, j * 2 + q)
                        act.activation(hid[:, 0, :], bank[4][:, 0:F], ACT.Exp, scale=-1.0).then_inc(s_ge, 1)
                        act.wait_ge(s_scat, j * 2 + q)
                        for n in range(2):
                            act.wait_ge(s_y, j * 4 + (2 * q + n + 1))
                            act.activation(ysb[:, q, 512 * n:512 * n + 512], bank[5 + n][:, :], ACT.Copy)\
                               .then_inc(s_ye, 1)
                act.wait_ge(s_acc, 1)
                for b in (2, 3):
                    act.activation(accsb[:, 2 * b:2 * b + 2, :], bank[b][:, :].rearrange("p (a t) -> p a t", a=2), ACT.Copy)\
                       .then_inc(s_aca, 1)

            @block.vector
            def _(dve):
                s = Chain(dve, s_dc2)
                norm_vector(dve, 1)
                norm_read_vector(dve, g_ffn, 1)
                s(dve.memset(lgp[:, :, NG:], -3e38))
                dve.wait_ge(s_wr, 64)
                dve.wait_ge(s_lg, 1)
                s(dve.tensor_tensor(lg, bank[4][:, 0:128].rearrange("p (t c) -> p t c", t=NT)[:, :, 0:NG + NE],
                                    rb.unsqueeze(1).broadcast_to([P, NT, NG + NE]), ALU.add))
                s.sync()
                s(dve.tensor_copy(lgp[:, :, 0:NG], lg[:, :, 0:NG]))
                s.sync()
                for t in range(NT):
                    s(dve.max(t8[:, t, :], lgp[:, t, :]))
                s.sync()
                for t in range(NT):
                    s(dve.max_index(i8[:, t, :].bitcast(U32), t8[:, t, :], lgp[:, t, :]))
                s.sync()
                for t in range(NT):
                    s(dve.tensor_copy(gf[:, t:t + 1], i8[:, t, 0:1].bitcast(U32)))
                    last = dve.tensor_scalar(lgp[:, t, 0:NG], lg[:, t, 0:NG], t8[:, t, 0:1], None, ALU.subtract)
                    if t == 0:
                        s(last)
                last.then_inc(s_rx, 1)
                s.sync()
                for t in range(NT):
                    s(dve.tensor_scalar(el[:, t, :], cst[:, K_GRP:K_GRP + NE], gf[:, t:t + 1], -BIG,
                                        ALU.not_equal, ALU.mult))
                s.sync()
                s(dve.tensor_tensor(el, el, lg[:, :, NG:], ALU.add))
                s.sync()
                for t in range(NT):
                    s(dve.max(t8[:, t, :], el[:, t, :]))
                s.sync()
                for t in range(NT):
                    s(dve.max_index(i8[:, t, :].bitcast(U32), t8[:, t, :], el[:, t, :]))
                s.sync()
                for t in range(NT):
                    s(dve.tensor_copy(gf[:, 2 + 2 * t:4 + 2 * t], i8[:, t, 0:2].bitcast(U32)))
                    last = dve.tensor_tensor(rw[:, 2 + t:3 + t], t8[:, t, 1:2], t8[:, t, 0:1], ALU.subtract)
                    if t == 0:
                        s(last)
                last.then_inc(s_rx, 1)
                dve.wait_ge(s_rxe, 1)
                s(dve.tensor_reduce(rw[:, 0:2], lgp[:, :, 0:NG], AX.X, ALU.add))
                dve.wait_ge(s_rxe, 2)
                s(dve.tensor_scalar(rw[:, 6:8], rw[:, 4:6], 1.0, None, ALU.add))
                s.sync()
                s(dve.tensor_tensor(rw[:, 6:8], rw[:, 6:8], rw[:, 0:2], ALU.mult))
                s.sync()
                s(dve.reciprocal(rw[:, 8:10], rw[:, 6:8]))
                s.sync()
                s(dve.tensor_tensor(rw[:, 10:12], rw[:, 8:10], rw[:, 4:6], ALU.mult))
                for t in range(NT):
                    for a in range(2):
                        s(dve.tensor_scalar(oh[:, a, :], cst[:, K_IOTA:K_IOTA + NE], gf[:, 2 + 2 * t + a:3 + 2 * t + a],
                                            None, ALU.is_equal))
                    s.sync()
                    s(dve.tensor_tensor(Msel[:, t, :], oh[:, 0, :], oh[:, 1, :], ALU.add))
                    s(dve.tensor_scalar(Wsel[:, t, :], oh[:, 0, :], rw[:, 8 + t:9 + t], None, ALU.mult))
                    s.sync()
                    last = dve.scalar_tensor_tensor(out=Wsel[:, t, :], in0=oh[:, 1, :], scalar=rw[:, 10 + t:11 + t],
                                                    in1=Wsel[:, t, :], op0=ALU.mult, op1=ALU.add)
                    if t == 0:
                        s(last)
                        s.sync()
                last.then_inc(s_sel, 1)
                dve.wait_ge(s_sel, 1)
                dve.wait_ge(s_rk, 1)
                s(dve.tensor_scalar(Rk, bank[5][:, 0:2 * NE].rearrange("p (t e) -> p t e", t=NT), 1.0, None, ALU.add))
                s.sync()
                s(dve.tensor_tensor(Rk, Rk, Msel, ALU.mult))
                s.sync()
                s(dve.tensor_scalar(Rk, Rk, -1.0, None, ALU.add))
                s(dve.tensor_reduce(cmax[:, 0:1], bank[5][:, 2 * NE:3 * NE], AX.X, ALU.max))
                s.sync()
                dve.tensor_scalar(ovf[:, :], cmax[:, 0:1], float(CAP), None, ALU.is_gt)
                slots = cst[:, K_IOTA:K_IOTA + CAP].unsqueeze(1).broadcast_to([P, NE, CAP])

                for t in range(NT):
                    dve.tensor_tensor(picked(t), slots, bc(Rk[:, t, :], [P, NE, CAP]), ALU.is_equal).then_inc(s_S, 1)

                def gathered(half, q):
                    dve.tensor_tensor(XT[:, q, 4 * half:4 * half + 4, :], bank[7 - half][:, :].rearrange("p (a c) -> p a c", a=4),
                                      bc(g_ffn[:, 4 * half:4 * half + 4], [P, 4, P]), ALU.mult).then_inc(s_xge, 1)

                dve.wait_ge(s_st, 1)
                dve.tensor_copy(STw[:, 1:5, 0:P], bank[4][:, :].rearrange("p (a c) -> p a c", a=4)).then_inc(s_std, 1)
                for half in range(2):
                    dve.wait_ge(s_xg, half + 1)
                    gathered(half, 0)
                dve.wait_ge(s_st, 3)
                dve.tensor_copy(STw[:, 1:5, P:T], bank[4][:, :].rearrange("p (a c) -> p a c", a=4)).then_inc(s_std, 1)
                with dve.Fori(0, NGRP // 2) as j:
                    for q in range(2):
                        s2 = Chain(dve, s_dch)
                        dve.sem_clear(s_dch)
                        dve.wait_ge(s_ge, j * 2 + (q + 1))
                        s2(dve.tensor_scalar(hid[:, 0, :], hid[:, 0, :], 1.0, None, ALU.add))
                        s2.sync()
                        s2(dve.reciprocal(hid[:, 1, :], hid[:, 0, :]))
                        s2.sync()
                        s2(dve.tensor_tensor(hid[:, 1, :], hid[:, 1, :], bank[4][:, 0:F], ALU.mult))
                        s2.sync()
                        dve.wait_ge(s_hdt, j * 2 + q)
                        dve.tensor_tensor(hid[:, 2, :], hid[:, 1, :], bank[4][:, F:2 * F], ALU.mult).then_inc(s_hd, 1)
                        for half in range(2):
                            dve.wait_ge(s_xg, j * 4 + (2 * q + 3 + half))
                            gathered(half, 1 - q)
                        dve.wait_ge(s_hdt, j * 2 + (q + 1))
                        dve.wait_ge(s_y, j * 4 + 2 * q)
                        dve.tensor_copy(hidT, bank[4][:, 0:2 * P].rearrange("p (a c) -> p a c", a=2)).then_inc(s_hde, 1)
                dve.wait_ge(s_acc, 1)
                for b in (0, 1):
                    dve.tensor_copy(accsb[:, 2 * b:2 * b + 2, :], bank[b][:, :].rearrange("p (a t) -> p a t", a=2))\
                       .then_inc(s_acd, 1)
                for i in range(4):
                    t, r = divmod(i, 2)
                    dve.wait_ge(s_fin, i + 1)
                    xi = x[:, t, 512 * r:512 * r + 512]
                    dve.tensor_tensor(xi, xi, bank[4 + i][:, :], ALU.add)

        over = nc.values_load(ovf[0:1, 0:1], min_val=0, max_val=1)
        with nc.If(over > 0):
            (o_sel, o_xg, o_xge, o_gu, o_ge, o_hd, o_hdt, o_hde, o_y, o_ye, o_st, o_wt, o_wte, o_sum) = s_o
            over_sems = range(s_ow.num, s_o[-1].num + 1)
            XO = XT[:, 0, :, 0:CAP]
            with nc.Fori(1, PASSES):
                with nc.Block() as block:
                    @block.vector
                    def _(dve):
                        dve.tensor_scalar(Rk, Rk, -float(CAP), None, ALU.add)
                with nc.Fori(0, NE) as ex:
                    with nc.Block() as block:
                        @block.sync
                        def _(sp):
                            for i in range(3):
                                expert_load(sp, layer, ex, i, ovw[:, i, :], s_ow)

                        @block.vector
                        def _(dve):
                            s = Chain(dve, o_st)
                            for t in range(NT):
                                s(dve.tensor_scalar(ovS[:, t, :], cst[:, K_IOTA:K_IOTA + CAP], Rk[:, t, bass.ds(ex, 1)],
                                                    None, ALU.is_equal))
                            s.sync()
                            for t in range(NT):
                                dve.tensor_scalar(ovW[:, t, :], ovS[:, t, :], Wsel[:, t, bass.ds(ex, 1)], None,
                                                  ALU.mult).then_inc(o_sel, 1)
                            dve.wait_ge(o_xg, 1)
                            dve.tensor_tensor(XO, bank[0][:, 0:KD * CAP].rearrange("p (a c) -> p a c", a=KD),
                                              bc(g_ffn, [P, KD, CAP]), ALU.mult).then_inc(o_xge, 1)
                            dve.wait_ge(o_wt, 1)
                            dve.tensor_copy(ovT[0:CAP, :], bank[5][0:CAP, 0:T]).then_inc(o_wte, 1)
                            dve.wait_ge(o_ge, 1)
                            s(dve.tensor_scalar(hid[0:CAP, 0, :], hid[0:CAP, 0, :], 1.0, None, ALU.add))
                            s.sync()
                            s(dve.reciprocal(hid[0:CAP, 1, :], hid[0:CAP, 0, :]))
                            s.sync()
                            s(dve.tensor_tensor(hid[0:CAP, 1, :], hid[0:CAP, 1, :], bank[1][0:CAP, 0:F], ALU.mult))
                            s.sync()
                            dve.tensor_tensor(hid[0:CAP, 2, :], hid[0:CAP, 1, :], bank[1][0:CAP, F:2 * F],
                                              ALU.mult).then_inc(o_hd, 1)
                            dve.wait_ge(o_hdt, 1)
                            dve.tensor_copy(hidT[:, :, 0:CAP], bank[2][:, 0:2 * CAP].rearrange("p (a c) -> p a c", a=2))\
                               .then_inc(o_hde, 1)
                            for i in range(4):
                                t, n = divmod(i, 2)
                                dve.wait_ge(o_sum, i + 1)
                                xi = x[:, t, 512 * n:512 * n + 512]
                                dve.tensor_tensor(xi, xi, bank[(6, 7, 0, 1)[i]][:, :], ALU.add)

                        @block.scalar
                        def _(act):
                            act.wait_ge(o_gu, 1)
                            act.activation(hid[0:CAP, 0, :], bank[1][0:CAP, 0:F], ACT.Exp, scale=-1.0).then_inc(o_ge, 1)
                            for n in range(2):
                                act.wait_ge(o_y, n + 1)
                                act.activation(ysb[0:CAP, 0, 512 * n:512 * n + 512], bank[3 + n][0:CAP, :], ACT.Copy)\
                                   .then_inc(o_ye, 1)

                        @block.tensor
                        def _(pe):
                            pe.wait_ge(o_sel, 2)
                            for k in range(KD):
                                for t in range(NT):
                                    last = pe.matmul(bank[0][:, k * CAP:(k + 1) * CAP], h2[:, t, k::KD], ovS[:, t, :],
                                                     start=(t == 0), stop=(t == NT - 1))
                            last.then_inc(o_xg, 1)
                            for t in range(NT):
                                last = pe.transpose(bank[5][0:CAP, t * P:(t + 1) * P], ovW[:, t, :], ident)
                            last.then_inc(o_wt, 1)
                            pe.wait_ge(s_ow, 48)
                            pe.wait_ge(o_xge, 1)
                            for k in range(KD):
                                last = pe.matmul(bank[1][0:CAP, :].rearrange("p (a f) -> p a f", a=2), XO[:, k, :],
                                                 ovw[:, 0:2, k * F:(k + 1) * F], start=(k == 0), stop=(k == KD - 1))
                            last.then_inc(o_gu, 1)
                            pe.wait_ge(o_hd, 1)
                            for a in range(2):
                                last = pe.transpose(bank[2][:, a * CAP:(a + 1) * CAP], hid[0:CAP, 2, a::2],
                                                    ident[0:CAP, 0:CAP])
                            last.then_inc(o_hdt, 1)
                            pe.wait_ge(o_hde, 1)
                            for n in range(2):
                                for a in range(2):
                                    last = pe.matmul(bank[3 + n][0:CAP, :], hidT[:, a, 0:CAP],
                                                     ovw[:, 2, a * D + 512 * n:a * D + 512 * n + 512],
                                                     start=(a == 0), stop=(a == 1))
                                last.then_inc(o_y, 1)
                            pe.wait_ge(o_ye, 2)
                            pe.wait_ge(o_wte, 1)
                            for i in range(4):
                                t, n = divmod(i, 2)
                                pe.matmul(bank[(6, 7, 0, 1)[i]][:, :], ovT[0:CAP, t * P:(t + 1) * P],
                                          ysb[0:CAP, 0, 512 * n:512 * n + 512], start=True, stop=True).then_inc(o_sum, 1)
                    nc.multi_engine_barrier(ALL, sems_to_clear=over_sems)
        nc.multi_engine_barrier(ALL, sems_to_clear=layer_sems)

    gfin = region(4096, D)
    f_ld = sem("final_gain_loaded")
    f_ss = sem("final_squares")
    f_st = sem("final_steps")
    f_rs = sem("final_rstd")
    f_o = sem("final_ready")
    with nc.Block() as block:
        @block.sync
        def _(sp):
            sp.dma_start(gfin, A["norm_final"].partition_broadcast(P)).then_inc(f_ld, 16)
            for t in range(NT):
                sp.wait_ge(f_o, t + 1)
                sp.dma_start(out[0, t * P:(t + 1) * P, :], hA[:, t, :]).then_inc(stored, 16)
            sp.wait_ge(stored, 16 * NT)

        @block.scalar
        def _(act):
            for t in range(NT):
                act.activation(hA[:, t, :], x[:, t, :], ACT.Square, accum_out=ss[:, t:t + 1]).then_inc(f_ss, 1)

        @block.gpsimd
        def _(pool):
            g = Chain(pool, f_st)
            pool.wait_ge(f_ss, NT)
            g(pool.tensor_scalar(ss[:, 2:4], ss[:, 0:2], 1.0 / D, EPS, ALU.mult, ALU.add))
            g.sync()
            pool.tensor_tensor(rstd[:, 0:2], ss[:, 2:4], rexp[:, 0:2], ALU.pow).then_inc(f_rs, 1)

        @block.vector
        def _(dve):
            dve.wait_ge(f_rs, 1)
            dve.wait_ge(f_ld, 16)
            for t in range(NT):
                dve.scalar_tensor_tensor(out=hA[:, t, :], in0=x[:, t, :], scalar=rstd[:, t:t + 1], in1=gfin,
                                         op0=ALU.mult, op1=ALU.mult).then_inc(f_o, 1)


_INS = ["x", "positions", "rel_bias", "norm_attn", "w_in", "b_merge", "cmp_pe", "cmp_k_w1", "cmp_k_b1", "cmp_k_w2",
        "cmp_v_w1", "cmp_v_b1", "cmp_v_w2", "mla_q_norm", "mla_kv_norm", "mla_w_uq", "mla_w_uk", "mla_w_uv", "fox_b_f",
        "w_o_nsa", "w_o_mla", "w_o_fox", "w_out", "norm_ffn", "moe_w_grp", "moe_b_grp", "moe_w_router",
        "moe_b_router", "moe_w_gate", "moe_w_up", "moe_w_down", "norm_final"]


def kernel(**inputs):
    import concourse.bacc as bacc
    from concourse.bass_utils import run_bass_kernel_spmd

    nc = bacc.Bacc("TRN2", target_bir_lowering=False, num_devices=1)
    arrays, aps = {}, {}
    consts = shape_constants()
    for name, a in [(n, inputs[n]) for n in _INS] + [("shape_c", consts[0]), ("shape_oh", consts[1])]:
        a = np.ascontiguousarray(a)
        arrays[f"in_{name}"] = a
        aps[name] = nc.dram_tensor(f"in_{name}", a.shape, mybir.dt.from_np(a.dtype), kind="ExternalInput").ap()
    out = nc.dram_tensor("out_0", (1, T, D), F32, kind="ExternalOutput").ap()
    build(nc, aps, out)
    r = run_bass_kernel_spmd(nc, [arrays], core_ids=[0])
    return r.results[0]["out_0"]
```

```python
from contextlib import ExitStack

import numpy as np

import concourse.bass as bass
from concourse import mybir
from concourse.alu_op_type import AluOpType as ALU

F32 = mybir.dt.float32
I32 = mybir.dt.int32
U32 = mybir.dt.uint32
ACT = mybir.ActivationFunctionType
AX = mybir.AxisListType
ENG = mybir.EngineType

P = 128
D = 1024
T = 256
NT = T // P
DEPTH = 2
KD = D // P
EPS = 1e-6
BIG = 1e30

H = 8
DH = 64
NQ = H * DH
QK = 96
ROPE = 32
HALF = ROPE // 2
CMP = 16
NCMP = T // CMP - 1
HID = 128

NE = 32
NG = 4
F = 256
CAP = 32
NGRP = NE // 4
PASSES = T // CAP

SLOTS = 12
SLOT = 2048
SPARE = 4
ATT_LOADS = 36
HROWS = 47
WARM, FILL = 14, 8
AHEAD = 5
ATT_TURNS = ATT_LOADS // SLOTS
MOE_SLOTS = SLOTS + SPARE
MOE_TURNS = 12 * NGRP // MOE_SLOTS
TURNS = ATT_TURNS + MOE_TURNS
assert ATT_LOADS % SLOTS == 0 and 12 * NGRP % MOE_SLOTS == 0 and 4 * 12 % MOE_SLOTS == 0

C_NQ, C_KC, C_KS, C_KW, C_G = 0, 512, 768, 1024, 1280
C_FQ, C_FK, C_FV, C_FF, C_MG = 1720, 2232, 2744, 3256, 3264
M_CQ, M_CKV, M_KR, M_FF, M_W = 24, 280, 408, 440, 448

L_MPA, L_MPB, L_NQ, L_KC, L_KS, L_KW, L_FQ, L_FK, L_FV, L_UQ, L_MRG, L_OUT = 0, 1, 2, 4, 5, 6, 7, 9, 11, 13, 14, 32

K_ID, K_TRI, K_ONES, K_STRICT, K_IOTA, K_HM, K_OK, K_MASK, K_INV, K_GRP, K_W = (
    0, 128, 256, 384, 512, 576, 584, 616, 872, 888, 920)
OH_W = 384


def shape_constants():
    p = np.arange(P)[:, None]
    j = np.arange(P)[None, :]
    c = np.zeros((P, K_W), np.float32)
    c[:, K_ID:K_ID + P] = p == j
    c[:, K_TRI:K_TRI + P] = j >= p
    c[:, K_ONES:K_ONES + P] = 1
    c[:, K_STRICT:K_STRICT + P] = j > p
    c[:, K_IOTA:K_IOTA + CAP] = np.arange(CAP)
    c[:, K_HM:K_HM + H] = (p // 16) == np.arange(H)[None, :]
    n = np.arange(16)[None, :]
    for t in range(NT):
        c[:, K_OK + 16 * t:K_OK + 16 * t + 16] = (t * P + p - (n * CMP + 31) >= 0) & (n < NCMP)
    c[:, K_MASK:K_MASK + T] = np.where(P + p - np.arange(T)[None, :] >= 0, 0, -8 * BIG)
    c[:, K_INV:K_INV + HALF] = np.float32(10000.0) ** (-np.arange(HALF, dtype=np.float32) / HALF)
    c[:, K_GRP:K_GRP + NE] = np.arange(NE) // (NE // NG)

    def onehot(dist, masked):
        n = np.maximum(dist, 0)
        ratio = np.log(np.maximum(n, 1).astype(np.float32) / np.float32(16)) / np.float32(np.log(8.0))
        large = 16 + (ratio.astype(np.float32) * np.float32(16)).astype(np.int32)
        b = np.where(n < 16, n, np.minimum(large, 31))
        o = np.zeros((33,) + dist.shape, np.float32)
        for i in range(32):
            o[i] = (b == i) & ~masked
        o[32] = masked
        return o

    x = (T - 1) - np.arange(OH_W)
    rev = onehot(x, x < 0)
    q = np.arange(P)[None, None, :] + P * np.arange(NT)[:, None, None]
    n = np.arange(16)[None, :, None]
    dc = q - (n * CMP + 31)
    oc = onehot(dc, (dc < 0) | (n >= NCMP)).reshape(33, -1)
    return c, np.concatenate([rev, oc], axis=1).astype(np.float32)


class Chain:

    def __init__(self, eng, sem):
        self.eng, self.sem, self.n = eng, sem, 0

    def __call__(self, ins):
        ins.then_inc(self.sem, 1)
        self.n += 1
        return self.n

    def sync(self, n=None):
        self.eng.wait_ge(self.sem, self.n if n is None else n)


def bc(ap, shape):
    while len(ap.shape) < len(shape):
        ap = ap.unsqueeze(len(ap.shape))
    return ap.broadcast_to(list(shape))


def build(nc, A, out):
    with ExitStack() as ctx:
        program(nc, A, out, ctx)


def program(nc, A, out, ctx):
    def sb(name, shape, dt=F32):
        return ctx.enter_context(nc.sbuf_tensor(name, shape, dt))

    def sem(name):
        return ctx.enter_context(nc.semaphore(name))

    bank = [ctx.enter_context(nc.psum_tensor(f"bank{i}", [P, 512], F32)) for i in range(8)]
    ring = sb("ring", [P, SLOTS, SLOT])
    x = sb("x_res", [P, NT, D])
    cst = sb("cst", [P, K_W])
    trig = sb("trig", [P, 2, NT, HALF])
    biasc = sb("biasc", [P, NT, H, 16])
    small = sb("small", [P, 700])
    AW = 24448
    arena = sb("arena", [P, AW])
    ident = cst[:, K_ID:K_ID + P]
    table = nc.dram_tensor("bias_table", [H, P, OH_W], F32, kind="Internal").ap()

    def region(at, *dims):
        n = int(np.prod(dims))
        assert at + n <= AW, (at, n)
        v = arena[:, at:at + n]
        if len(dims) == 2:
            v = v.rearrange("p (a b) -> p a b", b=dims[1])
        if len(dims) == 3:
            v = v.rearrange("p (a b c) -> p a b c", b=dims[1], c=dims[2])
        if len(dims) == 4:
            v = v.rearrange("p (a b c d) -> p a b c d", b=dims[1], c=dims[2], d=dims[3])
        return v

    def tiny(at, *dims):
        n = int(np.prod(dims))
        v = small[:, at:at + n]
        assert at + n <= 700
        if len(dims) == 2:
            v = v.rearrange("p (a b) -> p a b", b=dims[1])
        if len(dims) == 3:
            v = v.rearrange("p (a b c) -> p a b c", b=dims[1], c=dims[2])
        return v

    hT = region(0, KD, T)
    hA = region(2048, NT, D)
    mqT = region(2048, H, T)
    mixT = region(2048, KD, T)
    nqT = region(4096, 4, T)
    nkT = [region(5120, 2, T), region(22912, 2, T)]
    nv = region(5632, NT, 2, P)
    mp = region(6144, NT, M_W)
    fqT = region(7040, 4, T)
    fkT = region(8064, 4, T)
    fv = region(9088, NT, NQ)
    mkT = region(10112, H, T)
    mv = region(12160, NT, NQ)
    bias8 = region(13184, H, T)
    cqT = region(13184, 2, T)
    ckvT = region(13696, T)
    prob = [region(at, 2, 384) for at in (15232, 16000, 6144)]
    probT = region(16768, 2, 2, 384)
    cw1v = region(15232, 16, HID)
    vcbd = region(17280, H, DH)
    pc = region(17792, NT, P)
    pcT = region(18048, NT, P)
    of_ = region(18304, NT, NQ)
    om_ = region(19328, NT, NQ)
    on_ = region(20352, NT, NQ)
    qtm = region(18304, NT, H * QK)
    uv = region(19840, NQ)
    oT = region(21376, 3, 4, T)
    cw1k = region(20352, 16, HID)
    kcp = region(23424, 2, 3, P)
    hvr = region(24192, P)
    stage_b = region(24192, P)
    stage_pe = region(24320, P)
    hrow = region(17600, HID)
    cmpt = region(17280, 5, 64)
    bias0 = region(21376, H, P)
    krt = region(17792, 4, NT * HALF)
    qrt = region(2048, 4, NT * H * HALF)
    mexp = region(15232, 4, T)
    mtmp = region(16768, 2, T)
    otmp = region(22400, 512)
    h2 = region(2048, NT, D)
    Ssel = region(4096, NT, NGRP + 1, P)
    STw = region(6400, NGRP + 1, T)
    Sw = region(8704, NT, NE, CAP)
    XT = region(10752, 2, KD, P)
    ysb = region(12800, 2, D)
    hid = region(14848, 3, F)
    hidT = region(15616, 2, P)
    accsb = region(0, KD, T)
    ovw = region(4096, 3, SLOT)
    ovS = region(10240, NT, CAP)
    ovW = region(10368, NT, CAP)
    ovT = region(10496, T)
    wrt = region(15872, KD, NG + NE)
    spare = region(16256, SPARE, SLOT)
    g_att = tiny(0, KD)
    g_ffn = tiny(8, KD)
    g_q = tiny(16, 2)
    g_kv = tiny(18, 1)
    b1 = tiny(20, 2)
    nbm = tiny(22, 24)
    bf = tiny(46, H)
    w2k = tiny(54, 2, DH)
    w2v = tiny(182, DH)
    ss = tiny(246, 8)
    rstd = tiny(254, 8)
    rexp = tiny(680, 8)
    ng = tiny(270, NT, 24)
    mx = tiny(318, 64)
    sm = tiny(382, 64)
    coef = tiny(446, 64)
    hidc = tiny(510, 2, 32)
    kcT = tiny(574, 32)
    lf = tiny(606, NT, H)
    lft = tiny(622, 3, NT * H)
    rb = tiny(20, NG + NE)
    lg = tiny(56, NT, NG + NE)
    lgp = tiny(128, NT, 8)
    t8 = tiny(144, NT, 8)
    i8 = tiny(160, NT, 8)
    gf = tiny(176, 8)
    el = tiny(270, NT, NE)
    rw = tiny(334, 16)
    oh = tiny(350, 2, NE)
    Msel = tiny(414, NT, NE)
    Wsel = tiny(478, NT, NE)
    Rk = tiny(542, NT, NE)
    cmax = tiny(640, 2)
    ovf = sb("ovf", [P, 1], I32)
    left = sb("left", [P, 1], I32)
    pos_i = sb("pos_i", [P, NT], I32)

    landed = [sem(f"landed{i}") for i in range(MOE_SLOTS)]
    s_mpb = sem("forget_cols_loaded")
    s_uk = sem("uk_loaded")
    stored = sem("stored")
    first = {}

    def csem(name):
        first[name] = sem(name)
        return first[name]

    s_small = csem("small_loaded")
    s_cw1 = csem("compress_w_loaded")
    s_cw2 = csem("compress_w2_loaded")
    s_uv = csem("uv_loaded")
    s_bias = csem("bias_loaded")
    s_prep = csem("loads_transposed")
    s_ss = csem("squares_summed")
    s_rstd = csem("rstd_ready")
    s_h = csem("h_ready")
    s_ht = csem("h_transposed_psum")
    s_hTd = csem("hT_by_vector")
    s_hTa = csem("hT_by_scalar")
    s_proj = csem("projected")
    s_evd = csem("projection_read_by_vector")
    s_eva = csem("projection_read_by_scalar")
    s_ach = csem("scalar_steps")
    s_dch = csem("vector_steps")
    s_gch = csem("gpsimd_steps")
    s_gc2 = csem("gpsimd_expert_steps")
    s_lss = csem("latent_squares")
    s_lrstd = csem("latent_rstd")
    s_lat = csem("latent_normed")
    s_latp = csem("latent_transposed_psum")
    s_latT = csem("latent_transposed")
    s_kr = csem("rope_key_stored")
    s_mk = csem("latent_key_psum")
    s_mke = csem("latent_key_read")
    s_mq = csem("latent_q_psum")
    s_qr = csem("latent_q_rotated")
    s_mqt = csem("latent_qT_psum")
    s_mqte = csem("latent_qT_read")
    s_mv = csem("latent_v_psum")
    s_mve = csem("latent_v_read")
    s_gx = csem("gate_logits_exp")
    s_z = csem("forget_logits_ready")
    s_ln = csem("forget_softplus")
    s_gz = csem("gelu_exp_wanted")
    s_gexp = csem("gelu_exp")
    s_sx = csem("cmp_exp_wanted")
    s_sexp = csem("cmp_exp")
    s_pz = csem("pe_block_zeroed")
    s_lf = csem("log_forget_ready")
    s_fb = csem("cum_forget_psum")
    s_fbe = csem("cum_forget_read")
    s_hc = csem("hidden_rows_psum")
    s_hcs = csem("hidden_rows_read")
    s_hct = csem("hidden_psum")
    s_hid = csem("hidden_ready")
    s_kv = csem("compressed_psum")
    s_kcT = csem("compressed_ready")
    s_sc = csem("cmp_scores_psum")
    s_pc = csem("cmp_probs_ready")
    s_pct = csem("cmp_probsT_psum")
    s_pcT = csem("cmp_probsT_ready")
    s_oc = csem("cmp_out_psum")
    s_oce = csem("cmp_out_read")
    s_qk = csem("scores_psum")
    s_max = csem("scores_shifted")
    s_exp = csem("probs_ready")
    s_pt = csem("probsT_psum")
    s_pta = csem("probsT_ready")
    s_pv = csem("values_summed")
    s_oe = csem("branch_out_read")
    s_ot = csem("outT_psum")
    s_oTe = csem("outT_read_by_vector")
    s_oTa = csem("outT_read_by_scalar")
    s_mgl = csem("merge_logits_psum")
    s_mg = csem("merge_psum")
    s_mge = csem("merge_exp")
    s_mgd = csem("merge_read")
    s_op = csem("out_projected")
    s_wr = csem("router_w_loaded")
    s_lg = csem("logits_psum")
    s_rx = csem("router_exp_wanted")
    s_rxe = csem("router_exp")
    s_sel = csem("selected")
    s_rk = csem("ranks_psum")
    s_S = csem("selection_ready")
    s_sw = csem("weighted_selection")
    s_st = csem("selectionT_psum")
    s_std = csem("selectionT_read_by_vector")
    s_sta = csem("selectionT_read_by_scalar")
    s_yz = csem("zeros_ready")
    s_xg = csem("gathered_psum")
    s_xge = csem("gathered_read")
    s_gu = csem("gate_up_psum")
    s_ge = csem("gate_exp")
    s_hd = csem("expert_hidden")
    s_hdt = csem("expert_hiddenT_psum")
    s_hde = csem("expert_hiddenT_ready")
    s_y = csem("expert_out_psum")
    s_ye = csem("expert_out_read")
    s_dc2 = csem("vector_loop_steps")
    s_scat = csem("group_scattered")
    s_acc = csem("experts_summed")
    s_acd = csem("sum_read_by_vector")
    s_aca = csem("sum_read_by_scalar")
    s_fin = csem("sumT_psum")
    s_ow = csem("overflow_w_loaded")
    s_o = [csem(f"overflow_{n}") for n in
           ("selected", "gathered", "gathered_read", "gate_up", "gate_exp", "hidden", "hiddenT",
            "hiddenT_read", "out", "out_read", "steps", "weightT", "weightT_read", "summed")]
    nums = [s.num for s in first.values()]
    assert nums == list(range(nums[0], nums[-1] + 1)), nums
    layer_sems = range(nums[0], nums[-1] + 1)
    ALL = [ENG.DVE, ENG.Activation, ENG.PE, ENG.Pool, ENG.SP]

    def w_in_cols(layer, c0, n):
        return A["w_in"][layer].rearrange("(p k) c -> p k c", k=KD)[:, :, c0:c0 + n]

    def slot_cols(n, w):
        return ring[:, n % SLOTS, 0:KD * w].rearrange("p (k c) -> p k c", k=KD)

    def attention_load(sp, layer, n):
        done = landed[n % SLOTS]

        def whole(src, w=256):
            sp.dma_start(slot_cols(n, w), src).then_inc(done, 16)

        if n == L_MPA:
            whole(w_in_cols(layer, C_G, 256))
        elif n == L_MPB:
            sp.dma_start(slot_cols(n, 192)[:, :, 0:184], w_in_cols(layer, C_G + 256, 184)).then_inc(done, 16)
            sp.dma_start(slot_cols(n, 192)[:, :, 184:192], w_in_cols(layer, C_FF, 8)).then_inc(s_mpb, 16)
        elif n in (L_NQ, L_NQ + 1):
            whole(w_in_cols(layer, C_NQ + 256 * (n - L_NQ), 256))
        elif n in (L_KC, L_KS, L_KW):
            whole(w_in_cols(layer, {L_KC: C_KC, L_KS: C_KS, L_KW: C_KW}[n], 256))
        elif n < L_UQ:
            b = {0: C_FQ, 1: C_FK, 2: C_FV}[(n - L_FQ) // 2]
            whole(w_in_cols(layer, b + 256 * ((n - L_FQ) % 2), 256))
        elif n == L_UQ:
            sp.dma_start(ring[:, n % SLOTS, 0:1536],
                         A["mla_w_uq"][layer].rearrange("(p j) c -> p (j c)", j=2)).then_inc(done, 16)
            sp.dma_start(ring[:, n % SLOTS, 1536:2048], A["mla_w_uk"][layer]).then_inc(s_uk, 16)
        elif n < L_OUT:
            half, i = divmod(n - L_MRG, 9)
            if 3 <= i < 6:
                w = A[("w_o_nsa", "w_o_mla", "w_o_fox")[i - 3]][layer].rearrange("(c p) n -> p c n", c=4)
                sp.dma_start(ring[:, n % SLOTS, :].rearrange("p (c n) -> p c n", c=4),
                             w[:, :, 512 * half:512 * half + 512]).then_inc(done, 16)
            else:
                q, b = i // 6, i % 3
                whole(w_in_cols(layer, C_MG + b * D + 512 * half + 256 * q, 256))
        else:
            i = n - L_OUT
            whole(A["w_out"][layer].rearrange("(k p) n -> p k n", k=KD)[:, :, 256 * i:256 * i + 256])

    def expert_load(sp, layer, e, i, slot, done):
        if i < 2:
            src = A["moe_w_gate" if i == 0 else "moe_w_up"][layer, e].rearrange("(p k) f -> p (k f)", k=KD)
        else:
            src = A["moe_w_down"][layer, e].rearrange("(p j) n -> p (j n)", j=2)
        sp.dma_start(slot, src).then_inc(done, 16)

    GROUP = [(e, m) for e in range(4) for m in (0, 1)] + [(e, 2) for e in range(4)]

    ohs = arena[0:33, 0:OH_W + NT * 16 * P]
    rbe = small[0:33, 0:H]
    tabs = region(11000, OH_W)[0:H]
    ang = region(8192, 6, NT * HALF)
    u_ld = sem("setup_loaded")
    u_oh = sem("setup_bias_loaded")
    u_ms = sem("setup_mask_row")
    u_pe = sem("setup_psum")
    u_cp = sem("setup_copied")
    u_tb = sem("table_stored")
    u_ch = sem("setup_steps")
    u_sn = sem("setup_angles")
    with nc.Block() as block:
        @block.sync
        def _(sp):
            sp.dma_start(ohs, A["shape_oh"]).then_inc(u_oh, 16)
            sp.dma_start(x[:, :, :], A["x"][0].rearrange("(t p) d -> p t d", p=P)).then_inc(u_ld, 16)
            sp.dma_start(cst[:, :], A["shape_c"]).then_inc(u_ld, 16)
            for n in range(AHEAD):
                attention_load(sp, 0, n)

        @block.gpsimd
        def _(pool):
            pool.memset(small[32:33, 0:H], -BIG).then_inc(u_ms, 1)
            pool.wait_ge(u_ms, 1)
            pool.memset(rexp, -0.5)

        @block.tensor
        def _(pe):
            pe.wait_ge(u_oh, 32)
            pe.wait_ge(u_ms, 1)
            pe.matmul(bank[0][0:H, 0:OH_W], rbe, ohs[:, 0:OH_W], start=True, stop=True).then_inc(u_pe, 1)
            for t in range(NT):
                for n in range(16):
                    c = OH_W + (t * 16 + n) * P
                    last = pe.matmul(bank[1][:, (t * 16 + n) * H:(t * 16 + n + 1) * H], ohs[:, c:c + P], rbe,
                                     start=True, stop=True)
            last.then_inc(u_pe, 1)

        @block.scalar
        def _(act):
            act.dma_start(small[0:32, 0:H], A["rel_bias"]).then_inc(u_oh, 16)
            for t in range(NT):
                act.dma_start(pos_i[:, t:t + 1], A["positions"][0, t * P:(t + 1) * P].rearrange("(p o) -> p o", o=1))\
                   .then_inc(u_ld, 16)
            act.wait_ge(u_cp, 1)
            act.dma_start(table, tabs.unsqueeze(1).broadcast_to([H, P, OH_W])).then_inc(u_tb, 16)
            act.wait_ge(u_sn, 1)
            act.activation(trig[:, :, :, :], ang[:, 4:6, :].rearrange("p a (t i) -> p a t i", t=NT), ACT.Sin)

        @block.vector
        def _(dve):
            s = Chain(dve, u_ch)
            dve.wait_ge(u_ld, 64)
            dve.wait_ge(u_pe, 1)
            dve.tensor_scalar(tabs, bank[0][0:H, 0:OH_W], 8.0, None, ALU.mult).then_inc(u_cp, 1)
            s(dve.tensor_copy(small[:, 500:500 + NT], pos_i[:, :]))
            s.sync()
            for t in range(NT):
                s(dve.tensor_scalar(ang[:, 0, t * HALF:(t + 1) * HALF], cst[:, K_INV:K_INV + HALF],
                                    small[:, 500 + t:501 + t], None, ALU.mult))
            s.sync()
            MAGIC = float(1.5 * 2 ** 23)
            TWO_PI = 2 * np.pi
            HI, MID = 6.28125, 0.0019340515136718750
            LO = float(TWO_PI - HI - MID)
            for i, quarter in enumerate((0.25, 0.0)):
                s(dve.tensor_scalar(ang[:, 1, :], ang[:, 0, :], 1 / TWO_PI, quarter, ALU.mult, ALU.add))
                s.sync()
                s(dve.tensor_scalar(ang[:, 1, :], ang[:, 1, :], MAGIC, None, ALU.add))
                s.sync()
                s(dve.tensor_scalar(ang[:, 1, :], ang[:, 1, :], -MAGIC, None, ALU.add))
                s.sync()
                src = ang[:, 0, :]
                for part in (HI, MID, LO):
                    s(dve.scalar_tensor_tensor(out=ang[:, 2, :], in0=ang[:, 1, :], scalar=-part, in1=src,
                                               op0=ALU.mult, op1=ALU.add))
                    s.sync()
                    src = ang[:, 2, :]
                s(dve.tensor_scalar(ang[:, 2, :], ang[:, 2, :], quarter * TWO_PI, 3.1415925, ALU.add, ALU.min))
                s.sync()
                last = dve.tensor_scalar(ang[:, 4 + i, :], ang[:, 2, :], -3.1415925, None, ALU.max)
                if i == 0:
                    s(last)
                    s.sync()
            last.then_inc(u_sn, 1)
            dve.wait_ge(u_pe, 2)
            for t in range(NT):
                dve.tensor_scalar(biasc[:, t, :, :].rearrange("p h n -> p n h"),
                                  bank[1][:, 128 * t:128 * t + 128].rearrange("p (n h) -> p n h", h=H),
                                  8.0, None, ALU.mult)

    def norm_scalar(act):
        act.activation(hA[:, 0, :], x[:, 0, :], ACT.Square, accum_out=ss[:, 0:1]).then_inc(s_ss, 1)

    def norm_square(dve, done):
        dve.tensor_tensor_reduce(out=hA[:, 1, :], in0=x[:, 1, :], in1=x[:, 1, :], scale=1.0, scalar=0.0,
                                 op0=ALU.mult, op1=ALU.add, accum_out=ss[:, 1:2]).then_inc(done, 1)

    def picked(t):
        return Ssel[:, t, 0:NGRP, :].rearrange("p i (e c) -> p (i e) c", e=4)

    def norm_pool(pool, g, use):
        pool.wait_ge(s_ss, NT * (use + 1))
        g(pool.tensor_scalar(ss[:, 2:4], ss[:, 0:2], 1.0 / D, EPS, ALU.mult, ALU.add))
        g.sync()
        pool.tensor_tensor(rstd[:, 0:2], ss[:, 2:4], rexp[:, 0:2], ALU.pow).then_inc(s_rstd, 1)

    def norm_vector(dve, use):
        dve.wait_ge(s_rstd, use + 1)
        for t in range(NT):
            dve.tensor_scalar(hA[:, t, :], x[:, t, :], rstd[:, t:t + 1], None, ALU.mult).then_inc(s_h, 1)

    def norm_tensor(pe, src):
        for r in range(4):
            for j in range(2):
                for t in range(NT):
                    last = pe.transpose(bank[r][:, j * T + t * P:j * T + t * P + P],
                                        src[:, t, 2 * r + j::KD], ident)
            last.then_inc(s_ht, 1)

    def norm_ready(pe, k, use):
        pe.wait_ge(s_hTa if (k // 2) % 2 else s_hTd, 2 * use + k // 4 + 1)

    def norm_read_vector(dve, gain, use):
        for r in (0, 2):
            dve.wait_ge(s_ht, 4 * use + r + 1)
            dve.tensor_tensor(hT[:, 2 * r:2 * r + 2, :], bank[r][:, :].rearrange("p (j t) -> p j t", j=2),
                              bc(gain[:, 2 * r:2 * r + 2], [P, 2, T]), ALU.mult).then_inc(s_hTd, 1)

    def norm_read_scalar(act, gain, use):
        for r in (1, 3):
            act.wait_ge(s_ht, 4 * use + r + 1)
            for j in range(2):
                last = act.activation(hT[:, 2 * r + j, :], bank[r][:, j * T:(j + 1) * T], ACT.Copy,
                                      scale=gain[:, 2 * r + j:2 * r + j + 1])
            last.then_inc(s_hTa, 1)

    JOBS = L_UQ
    UNITS = 16
    FOX, MLA, SLC, WIN = range(4)

    def jobs_read(pe, n):
        pe.wait_ge(s_eva if n % 2 else s_evd, n // 2 + 1)

    def score_cols(u, t, half):
        return (u // 2) * 8 + t * 4 + (u % 2) * 2 + half

    def seg(t):
        return (0, P) if t == 0 else (P, P + T)

    with nc.Fori(0, DEPTH) as layer:
        def ring_wait(eng, n):
            eng.wait_ge(landed[n % SLOTS], (layer * TURNS + (n // SLOTS + 1)) * 16)

        with nc.Block() as block:
            @block.sync
            def _(sp):
                small_loads = [
                    (g_att, A["norm_attn"][layer].rearrange("(p k) -> p k", k=KD)),
                    (g_ffn, A["norm_ffn"][layer].rearrange("(p k) -> p k", k=KD)),
                    (g_q, A["mla_q_norm"][layer].rearrange("(p k) -> p k", k=2)),
                    (g_kv, A["mla_kv_norm"][layer].rearrange("(p k) -> p k", k=1)),
                    (b1[:, 0:1], A["cmp_k_b1"][layer].rearrange("(p k) -> p k", k=1)),
                    (b1[:, 1:2], A["cmp_v_b1"][layer].rearrange("(p k) -> p k", k=1)),
                    (bf, A["fox_b_f"][layer].partition_broadcast(P)),
                    (stage_b[0:24, :], A["b_merge"][layer].rearrange("(c p) -> c p", p=P)),
                    (stage_pe[0:16, :], A["cmp_pe"][layer].rearrange("(m a) d -> m (a d)", a=2)),
                ]
                for dst, src in small_loads:
                    sp.dma_start(dst, src).then_inc(s_small, 16)
                for n in range(AHEAD, L_FQ):
                    attention_load(sp, layer, n)
                sp.dma_start(cw1k, A["cmp_k_w1"][layer].rearrange("(m p) h -> p m h", p=P), max_dma_last_dim=512).then_inc(s_cw1, 16)
                sp.dma_start(cw1v, A["cmp_v_w1"][layer].rearrange("(m p) h -> p m h", p=P), max_dma_last_dim=512).then_inc(s_cw1, 16)
                for i in range(2):
                    sp.dma_start(w2k[:, i, :], A["cmp_k_w2"][layer]).then_inc(s_cw2, 16)
                sp.dma_start(w2v, A["cmp_v_w2"][layer]).then_inc(s_cw2, 16)
                sp.dma_start(uv, A["mla_w_uv"][layer]).then_inc(s_uv, 16)
                for n in range(L_FQ, SLOTS):
                    attention_load(sp, layer, n)
                for n in range(SLOTS, ATT_LOADS + SLOTS):
                    m = n - SLOTS
                    if m < L_UQ:
                        sp.wait_ge(s_proj, m + 1)
                    elif m == L_UQ:
                        sp.wait_ge(s_mq, 4)
                        sp.wait_ge(s_mk, 4)
                    elif m < L_OUT:
                        half, i = divmod(m - L_MRG, 9)
                        sp.wait_ge(s_mg, 12 * half + (4 if i < 3 else 10) + i % 3)
                    else:
                        sp.wait_ge(s_op, m - L_OUT + 1)
                        if m == L_OUT:
                            sp.dma_start(wrt[:, :, 0:NG], A["moe_w_grp"][layer].rearrange("(p k) g -> p k g", k=KD)).then_inc(s_wr, 16)
                            sp.dma_start(wrt[:, :, NG:], A["moe_w_router"][layer].rearrange("(p k) g -> p k g", k=KD)).then_inc(s_wr, 16)
                            sp.dma_start(rb[:, 0:NG], A["moe_b_grp"][layer].partition_broadcast(P)).then_inc(s_wr, 16)
                            sp.dma_start(rb[:, NG:], A["moe_b_router"][layer].partition_broadcast(P)).then_inc(s_wr, 16)
                    if n < ATT_LOADS:
                        attention_load(sp, layer, n)
                    else:
                        i = n - ATT_LOADS
                        expert_load(sp, layer, GROUP[i][0], GROUP[i][1], ring[:, n % SLOTS, :],
                                    landed[n % SLOTS])
                    if m == L_UQ:
                        sp.wait_ge(u_tb, 16)
                        sp.wait_ge(s_max, 4)
                        sp.dma_start(bias8, bass.AP(table.tensor, P - 1, [[OH_W - 1, P], [P * OH_W, H], [1, T]]))\
                          .then_inc(s_bias, 16)

            @block.gpsimd
            def _(pool):
                g = Chain(pool, s_gch)
                pool.memset(kcp[:, :, 2, :], 0.0).then_inc(s_pz, 1)
                pool.wait_ge(s_pz, 1)
                norm_pool(pool, g, 0)
                pool.wait_ge(s_rstd, 1)
                pool.wait_ge(s_lss, 4)
                g(pool.tensor_scalar(ss[:, 2:4], ss[:, 4:6], 1.0 / 256, EPS, ALU.mult, ALU.add))
                g.sync()
                g(pool.tensor_scalar(ss[:, 0:2], ss[:, 6:8], 1.0 / P, EPS, ALU.mult, ALU.add))
                g.sync()
                pool.tensor_tensor(rstd[:, 2:4], ss[:, 2:4], rexp[:, 0:2], ALU.pow).then_inc(s_lrstd, 1)
                pool.wait_ge(s_lrstd, 1)
                pool.tensor_tensor(rstd[:, 4:6], ss[:, 0:2], rexp[:, 0:2], ALU.pow).then_inc(s_lrstd, 1)

            @block.tensor
            def _(pe):
                def keep_warm(n, b):
                    for _ in range(n):
                        pe.matmul(b[:, 0:P], ident, ident, start=True, stop=True)

                keep_warm(WARM, bank[7])
                pe.wait_ge(s_h, NT)
                norm_tensor(pe, hA)
                pe.wait_ge(s_small, 9 * 16)
                pe.transpose(bank[4][:, 0:24], stage_b[0:24, :], ident[0:24, 0:24])
                pe.transpose(bank[4][:, 32:48], stage_pe[0:16, :], ident[0:16, 0:16]).then_inc(s_prep, 1)

                def columns(dst, weight):
                    for k in range(KD):
                        last = pe.matmul(dst, weight(k), hT[:, k, :], start=(k == 0), stop=(k == KD - 1))
                    return last

                def rows(dst, t, weight):
                    for k in range(KD):
                        last = pe.matmul(dst, hT[:, k, t * P:(t + 1) * P], weight(k),
                                         start=(k == 0), stop=(k == KD - 1))
                    return last

                def compression_hidden():
                    pe.wait_ge(s_cw1, 32)
                    pe.wait_ge(s_evd, L_KC // 2 + 1)
                    for m in range(16):
                        for kv, w in enumerate((cw1k, cw1v)):
                            last = pe.matmul(bank[4][64 * kv:64 * kv + HROWS, 0:HID],
                                             kcp[:, kv].rearrange("p g n -> p (g n)")[:, m:m + 8 * (HROWS - 1) + 1:8],
                                             w[:, m, :], start=(m == 0), stop=(m == 15))
                    last.then_inc(s_hc, 1)
                    pe.wait_ge(s_lat, 1)
                    for j in range(2):
                        for t in range(NT):
                            pe.transpose(bank[5][:, (j * NT + t) * P:(j * NT + t + 1) * P],
                                         mp[:, t, M_CQ + j:M_CKV:2], ident)
                    for t in range(NT):
                        pe.transpose(bank[6][:, t * P:(t + 1) * P], mp[:, t, M_CKV:M_KR], ident)
                    for t in range(NT):
                        last = pe.transpose(bank[6][0:ROPE, T + t * P:T + (t + 1) * P], mp[:, t, M_KR:M_FF], ident)
                    last.then_inc(s_latp, 1)
                    pe.wait_ge(s_hcs, 1)
                    for kv in range(2):
                        r = slice(64 * kv, 64 * kv + HROWS)
                        last = pe.transpose(bank[(4, 7)[kv]][:, T:T + HROWS], hrow[r, :], ident[r, r])
                    last.then_inc(s_hct, 1)

                def compression_out():
                    pe.wait_ge(s_cw2, 48)
                    pe.wait_ge(s_hid, 1)
                    pe.matmul(bank[7][:, 0:32], w2k.rearrange("p a d -> p (a d)"), hidc[:, 0, :], start=True, stop=True)
                    pe.matmul(bank[7][:, 64:128], hvr, w2v, start=True, stop=True).then_inc(s_kv, 1)

                for n in range(JOBS):
                    ring_wait(pe, n)
                    if n == L_MPB:
                        pe.wait_ge(s_mpb, (layer + 1) * 16)
                    if n >= 4:
                        jobs_read(pe, n - 4)
                    b = bank[n % 4][:, :].rearrange("p (a c) -> p a c", a=2)
                    w = slot_cols(n, 192 if n == L_MPB else 256)
                    if n == 0:
                        for k in range(KD):
                            if k % 2 == 0:
                                norm_ready(pe, k, 0)
                            for a in range(2):
                                last = pe.matmul(b[:, a, :], hT[:, k, a * P:(a + 1) * P], w[:, k, :],
                                                 start=(k == 0 and a == 0), stop=(k == KD - 1), skip_group_check=True)
                        last.then_inc(s_proj, 1)
                        continue
                    for a in range(2):
                        if n in (L_NQ, L_NQ + 1, L_KC) or L_FQ <= n < L_FV:
                            last = columns(b[:, a, :], lambda k: w[:, k, a * P:(a + 1) * P])
                        elif n in (L_KS, L_KW):
                            if a == 0:
                                last = columns(b[:, 0, :], lambda k: w[:, k, 0:P])
                            else:
                                for t in range(NT):
                                    last = rows(b[:, 1, t * P:(t + 1) * P], t, lambda k: w[:, k, P:2 * P])
                        else:
                            wide = 192 if n == L_MPB else 256
                            last = rows(b[:, a, 0:wide], a, lambda k: w[:, k, 0:wide])
                    last.then_inc(s_proj, 1)
                    if n == L_FQ:
                        compression_hidden()
                    if n == L_FQ + 2:
                        compression_out()

                ring_wait(pe, L_UQ)
                pe.wait_ge(s_uk, (layer + 1) * 16)
                pe.wait_ge(s_latT, 2)
                for n in range(JOBS - 4, JOBS):
                    jobs_read(pe, n)
                uq = ring[:, L_UQ % SLOTS, 0:1536].rearrange("p (j c) -> p j c", j=2)
                for i in range(4):
                    t, hf = divmod(i, 2)
                    for j in range(2):
                        last = pe.matmul(bank[i][:, 0:384], cqT[:, j, t * P:(t + 1) * P],
                                         uq[:, j, 384 * hf:384 * hf + 384], start=(j == 0), stop=(j == 1))
                    last.then_inc(s_mq, 1)
                pe.wait_ge(s_kr, 1)
                for i in range(4):
                    if i >= 2:
                        pe.wait_ge(s_mke, i - 1)
                    for a in range(2):
                        h = 2 * i + a
                        last = pe.matmul(bank[5 + i % 2][0:DH, a * T:(a + 1) * T],
                                         ring[:, L_UQ % SLOTS, 1536 + DH * h:1536 + DH * h + DH], ckvT,
                                         start=True, stop=True)
                    last.then_inc(s_mk, 1)
                pe.wait_ge(s_uv, 16)
                pe.wait_ge(s_kcT, 1)
                for t in range(NT):
                    pe.matmul(bank[(4, 7)[t]][:, :], ckvT[:, t * P:(t + 1) * P], uv, start=True, stop=True)\
                      .then_inc(s_mv, 1)
                pe.wait_ge(s_mke, 4)
                for t in range(NT):
                    for c in range(4):
                        for half in range(2):
                            r = slice(DH * half, DH * half + DH)
                            last = pe.matmul(bank[5 + half][:, (t * 4 + c) * 16:(t * 4 + c + 1) * 16],
                                             nqT[r, c, t * P:(t + 1) * P], kcT[r, 16 * (c // 2):16 * (c // 2) + 16],
                                             start=True, stop=True)
                last.then_inc(s_sc, 1)
                pe.wait_ge(s_qr, 1)
                for i in range(4):
                    for a in range(2):
                        h = 2 * i + a
                        for t in range(NT):
                            last = pe.transpose(bank[i][0:QK, (a * NT + t) * P:(a * NT + t + 1) * P],
                                                qtm[:, t, QK * h:QK * h + QK], ident)
                    last.then_inc(s_mqt, 1)
                pe.wait_ge(s_mve, 2)
                pe.wait_ge(s_lf, 1)
                for i in range(4):
                    if i >= 2:
                        pe.wait_ge(s_fbe, i - 1)
                    b = bank[(4, 7)[i % 2]]
                    for a in range(2):
                        h = 2 * i + a
                        pe.matmul(b[:, a * T:(a + 1) * T], lf[:, 0, h:h + 1].broadcast_to([P, P]),
                                  cst[:, K_TRI:K_TRI + T], start=True, stop=False, skip_group_check=True)
                        last = pe.matmul(b[:, a * T + P:(a + 1) * T], lf[:, 1, h:h + 1].broadcast_to([P, P]),
                                         cst[:, K_TRI:K_TRI + P], start=False, stop=True, skip_group_check=True)
                    last.then_inc(s_fb, 1)
                pe.wait_ge(s_pc, 1)
                for t in range(NT):
                    last = pe.transpose(bank[5][:, t * P:(t + 1) * P], pc[:, t, :], ident)
                last.then_inc(s_pct, 1)
                pe.wait_ge(s_pcT, 1)
                for t in range(NT):
                    pe.matmul(bank[6 - t][:, :], pcT[:, t, :], vcbd.rearrange("p h d -> p (h d)"),
                              start=True, stop=True).then_inc(s_oc, 1)

                def operands(u):
                    br, c = divmod(u, 4)
                    for half in range(2):
                        r = slice(DH * half, DH * half + DH)
                        h = 2 * c + half
                        if br == FOX:
                            yield half, fqT[r, c, :], fkT[r, c, :], [fv[:, t, DH * h:DH * h + DH] for t in range(NT)]
                        elif br == MLA:
                            yield half, mqT[0:QK, h, :], mkT[0:QK, h, :], [mv[:, t, DH * h:DH * h + DH] for t in range(NT)]
                        else:
                            g = slice(DH * (c // 2), DH * (c // 2) + DH)
                            yield half, nqT[r, c, :], nkT[br - SLC][r, c // 2, :], [nv[:, t, br - SLC, g] for t in range(NT)]

                def scores(u):
                    if u >= 2:
                        pe.wait_ge(s_max, u - 1)
                    for t in range(NT):
                        for half, q, k, _v in operands(u):
                            lo, hi = seg(t)
                            last = pe.matmul(bank[2 * (u % 2) + half][:, lo:hi], q[:, t * P:(t + 1) * P],
                                             k[:, 0:hi - lo], start=True, stop=True)
                    last.then_inc(s_qk, 1)

                def turn(u):
                    pe.wait_ge(s_exp, u + 1)
                    if u:
                        pe.wait_ge(s_pta, u)
                    for half in range(2):
                        for i in range(3):
                            last = pe.transpose(bank[4 + half][:, i * P:(i + 1) * P],
                                                prob[u % 3][:, half, i * P:(i + 1) * P], ident)
                        last.then_inc(s_pt, 1)

                def values(u):
                    pe.wait_ge(s_pta, u + 1)
                    g = u // 2
                    if u % 2 == 0 and g >= 2:
                        pe.wait_ge(s_oe, g - 1)
                    o = bank[6 + g % 2][:, :].rearrange("p (t i d) -> p t i d", t=NT, i=4)
                    for half, _q, _k, v in operands(u):
                        i = (u % 2) * 2 + half
                        pt = probT[:, u % 2, half, :]
                        pe.matmul(o[:, 0, i, :], pt[:, 0:P], v[0], start=True, stop=True)
                        pe.matmul(o[:, 1, i, :], pt[:, P:2 * P], v[0], start=True, stop=False)
                        last = pe.matmul(o[:, 1, i, :], pt[:, 2 * P:3 * P], v[1], start=False, stop=True)
                    last.then_inc(s_pv, 1)

                pe.wait_ge(s_fbe, 4)
                keep_warm(FILL, bank[4])
                pe.wait_ge(s_mqte, 4)
                pe.wait_ge(s_oce, 2)
                def merge_loads(q):
                    m, b = divmod(q, 3)
                    return L_MRG + 9 * (m // 4) + 3 + b, L_MRG + 9 * (m // 4) + 6 * ((m // 2) % 2) + b

                def gate_logits(q):
                    m, lm = q // 3, merge_loads(q)[1]
                    if m % 2 == 0:
                        ring_wait(pe, lm)
                    wm = slot_cols(lm, 256)
                    columns(bank[q % 4][:, 0:T], lambda k: wm[:, k, (m % 2) * P:(m % 2 + 1) * P]).then_inc(s_mgl, 1)

                scores(0)
                scores(1)
                for u in range(UNITS):
                    if u + 2 < UNITS:
                        scores(u + 2)
                    if u == UNITS - 2:
                        pe.wait_ge(s_max, UNITS - 1)
                        gate_logits(0)
                    turn(u)
                    if u >= 1:
                        values(u - 1)
                    if u == UNITS - 2:
                        gate_logits(1)
                pe.wait_ge(s_max, UNITS)
                gate_logits(2)
                values(UNITS - 1)
                gate_logits(3)

                for n, i in enumerate((2, 3, 4, 5, 0, 1)):
                    src = (on_, om_, of_)[i // 2]
                    if n == 0:
                        pe.wait_ge(s_pta, UNITS)
                    elif n == 2:
                        pe.wait_ge(s_oe, 7)
                    elif n == 3:
                        pe.wait_ge(s_oTe, 1)
                    elif n == 4:
                        pe.wait_ge(s_oTa, 1)
                        pe.wait_ge(s_oe, 8)
                    elif n == 5:
                        pe.wait_ge(s_oTe, 2)
                    for a in range(2):
                        c = 2 * (i % 2) + a
                        for t in range(NT):
                            last = pe.transpose(bank[4 + n % 3][:, (a * NT + t) * P:(a * NT + t + 1) * P],
                                                src[:, t, c * P:(c + 1) * P], ident)
                    last.then_inc(s_ot, 1)
                pe.wait_ge(s_oTe, 3)
                pe.wait_ge(s_oTa, 3)
                for q in range(24):
                    m, b = divmod(q, 3)
                    lo = merge_loads(q)[0]
                    if m % 4 == 0:
                        ring_wait(pe, lo)
                    if q >= 4:
                        pe.wait_ge(s_mgd, q - 3)
                        gate_logits(q)
                    wo = ring[:, lo % SLOTS, :].rearrange("p (c n) -> p c n", c=4)
                    for c in range(4):
                        last = pe.matmul(bank[4 + q % 4][:, 0:T], wo[:, c, (m % 4) * P:(m % 4 + 1) * P],
                                         oT[:, b, c, :], start=(c == 0), stop=(c == 3))
                    last.then_inc(s_mg, 1)
                pe.wait_ge(s_mgd, 24)
                for i in range(4):
                    ring_wait(pe, L_OUT + i)
                    w = slot_cols(L_OUT + i, 256)
                    for t in range(NT):
                        for k in range(KD):
                            last = pe.matmul(bank[4 + i][:, t * T:(t + 1) * T], mixT[:, k, t * P:(t + 1) * P],
                                             w[:, k, :], start=(k == 0), stop=(k == KD - 1))
                    last.then_inc(s_op, 1)

            @block.scalar
            def _(act):
                s = Chain(act, s_ach)
                norm_scalar(act)
                act.wait_ge(s_small, 9 * 16)
                norm_read_scalar(act, g_att, 0)

                def read(n, dst, src):
                    act.wait_ge(s_proj, n + 1)
                    act.activation(dst, src, ACT.Copy).then_inc(s_eva, 1)

                two = lambda b: b[:, :].rearrange("p (a c) -> p a c", a=2)
                read(1, mp[:, :, 256:448], two(bank[1])[:, :, 0:192])
                act.wait_ge(s_evd, 1)
                act.wait_ge(s_eva, 1)
                for t in range(NT):
                    act.activation(of_[:, t, 0:256], mp[:, t, M_CQ:M_CKV], ACT.Square,
                                   accum_out=ss[:, 4 + t:5 + t]).then_inc(s_lss, 1)
                    act.activation(of_[:, t, 256:384], mp[:, t, M_CKV:M_KR], ACT.Square,
                                   accum_out=ss[:, 6 + t:7 + t]).then_inc(s_lss, 1)
                read(3, nqT[:, 2:4, :], two(bank[3]))
                act.activation(ng, mp[:, :, 0:24], ACT.Exp, scale=-1.0).then_inc(s_gx, 1)
                act.wait_ge(s_z, 1)
                s(act.activation(lft[:, 2, :], lft[:, 1, :], ACT.Exp, scale=-1.0))
                s.sync()
                act.activation(lft[:, 1, :], lft[:, 2, :], ACT.Ln, bias=1.0).then_inc(s_ln, 1)
                act.wait_ge(s_proj, L_KS + 1)
                for g in range(2):
                    for half in range(2):
                        act.activation(nkT[0][DH * half:DH * half + DH, g, :], bank[1][DH * g:DH * g + DH, 0:T], ACT.Copy)
                act.activation(nv[:, :, 0, :], two(bank[1])[:, 1, :].rearrange("p (t d) -> p t d", t=NT), ACT.Copy)\
                   .then_inc(s_eva, 1)
                read(7, fqT[:, 0:2, :], two(bank[3]))
                act.wait_ge(s_gz, 1)
                act.activation(cmpt[:, 2, :], cmpt[:, 1, :], ACT.Exp, scale=-2 * 0.7978845608028654)\
                   .then_inc(s_gexp, 1)
                read(9, fkT[:, 0:2, :], two(bank[1]))
                act.wait_ge(s_latp, 1)
                act.wait_ge(s_latT, 2)
                act.wait_ge(u_tb, 16)
                act.activation(mkT[DH:QK, :, :], bank[6][0:ROPE, T:2 * T].unsqueeze(1).broadcast_to([ROPE, H, T]),
                               ACT.Copy).then_inc(s_kr, 1)
                read(11, fv[:, :, 0:256], two(bank[3]))
                for i in range(4):
                    act.wait_ge(s_mk, i + 1)
                    act.activation(mkT[0:DH, 2 * i:2 * i + 2, :],
                                   bank[5 + i % 2][0:DH, :].rearrange("p (a t) -> p a t", a=2), ACT.Copy)\
                       .then_inc(s_mke, 1)
                for t in range(NT):
                    act.wait_ge(s_mv, t + 1)
                    act.activation(mv[:, t, :], bank[(4, 7)[t]][:, :], ACT.Copy).then_inc(s_mve, 1)
                act.wait_ge(s_sx, 1)
                act.activation(pc, pc, ACT.Exp, scale=0.125).then_inc(s_sexp, 1)
                for i in range(4):
                    act.wait_ge(s_mqt, i + 1)
                    act.activation(mqT[0:QK, 2 * i:2 * i + 2, :],
                                   bank[i][0:QK, :].rearrange("p (a t) -> p a t", a=2), ACT.Copy)\
                       .then_inc(s_mqte, 1)
                act.wait_ge(s_pct, 1)
                act.activation(pcT.rearrange("p t q -> p (t q)"), bank[5][:, 0:T], ACT.Copy).then_inc(s_pcT, 1)
                for t in range(NT):
                    act.wait_ge(s_oc, t + 1)
                    act.activation(on_[:, t, :], bank[6 - t][:, :], ACT.Copy).then_inc(s_oce, 1)
                for u in range(UNITS + 1):
                    if u < UNITS:
                        scale = QK ** -0.5 if u // 4 == MLA else DH ** -0.5
                        act.wait_ge(s_max, u + 1)
                        for half in range(2):
                            for t in range(NT):
                                lo, hi = seg(t)
                                c = score_cols(u, t, half)
                                pr = prob[u % 3][:, half, lo:hi]
                                last = act.activation(pr, pr, ACT.Exp, scale=scale, bias=mx[:, c:c + 1],
                                                      accum_out=sm[:, c:c + 1])
                        last.then_inc(s_exp, 1)
                    if u >= 1:
                        act.wait_ge(s_pt, 2 * u)
                        if u >= 3:
                            act.wait_ge(s_pv, u - 2)
                        for half in range(2):
                            last = act.activation(probT[:, (u - 1) % 2, half, :], bank[4 + half][:, 0:384], ACT.Copy)
                        last.then_inc(s_pta, 1)
                for n, i in ((1, 3), (3, 5), (5, 1)):
                    act.wait_ge(s_ot, n + 1)
                    act.activation(oT[:, i // 2, 2:4, :], two(bank[4 + n % 3]), ACT.Copy).then_inc(s_oTa, 1)
                for q in range(24):
                    m, b = divmod(q, 3)
                    act.wait_ge(s_mgl, q + 1)
                    if q >= 4:
                        act.wait_ge(s_mgd, q - 3)
                    act.activation(mexp[:, q % 4, :], bank[q % 4][:, 0:T], ACT.Exp, scale=-1.0,
                                   bias=nbm[:, b * KD + m:b * KD + m + 1]).then_inc(s_mge, 1)

            @block.vector
            def _(dve):
                s = Chain(dve, s_dch)
                two = lambda b: b[:, :].rearrange("p (a c) -> p a c", a=2)
                norm_square(dve, s_ss)
                norm_vector(dve, 0)
                dve.wait_ge(s_small, 9 * 16)
                norm_read_vector(dve, g_att, 0)
                dve.wait_ge(s_prep, 1)
                dve.wait_ge(s_pz, 1)
                dve.tensor_scalar(nbm, bank[4][:, 0:24], -1.0, None, ALU.mult)
                for kv in range(2):
                    last = dve.tensor_copy(kcp[:, kv, 2, 0:16], bank[4][:, 32:48])
                s(last)

                def read(n, dst, src):
                    dve.wait_ge(s_proj, n + 1)
                    dve.tensor_copy(dst, src).then_inc(s_evd, 1)

                read(0, mp[:, :, 0:256], two(bank[0]))
                read(2, nqT[:, 0:2, :], two(bank[2]))
                dve.wait_ge(s_eva, 1)
                z = lft[:, 0, :].rearrange("p (t h) -> p t h", t=NT)
                s(dve.tensor_tensor(z, mp[:, :, M_FF:M_W], bf.unsqueeze(1).broadcast_to([P, NT, H]), ALU.add))
                s.sync()
                s(dve.tensor_scalar(lft[:, 2, :], lft[:, 0, :], -1.0, None, ALU.mult))
                s.sync()
                dve.tensor_tensor(lft[:, 1, :], lft[:, 0, :], lft[:, 2, :], ALU.max).then_inc(s_z, 1)
                dve.wait_ge(s_lrstd, 2)
                for t in range(NT):
                    s(dve.tensor_scalar(mp[:, t, M_CQ:M_CKV], mp[:, t, M_CQ:M_CKV], rstd[:, 2 + t:3 + t], None, ALU.mult))
                    s(dve.tensor_scalar(mp[:, t, M_CKV:M_KR], mp[:, t, M_CKV:M_KR], rstd[:, 4 + t:5 + t], None, ALU.mult))
                k1, k2 = mp[:, :, M_KR:M_KR + HALF], mp[:, :, M_KR + HALF:M_FF]
                cos, sin = trig[:, 0], trig[:, 1]
                prod = [krt[:, i, :].rearrange("p (t c) -> p t c", t=NT) for i in range(4)]
                for i, (a, b) in enumerate(((k1, cos), (k2, sin), (k1, sin), (k2, cos))):
                    s(dve.tensor_tensor(prod[i], a, b, ALU.mult))
                s.sync()
                s(dve.tensor_tensor(k1, prod[0], prod[1], ALU.subtract))
                dve.tensor_tensor(k2, prod[2], prod[3], ALU.add).then_inc(s_lat, 1)
                dve.wait_ge(s_proj, L_KC + 1)
                for par in range(2):
                    for g in range(2):
                        last = dve.tensor_copy(kcp[DH * par:DH * par + DH, :, g, :],
                                               two(bank[L_KC % 4])[DH * g:DH * g + DH, :, par::2])
                last.then_inc(s_evd, 1)
                dve.wait_ge(s_gx, 1)
                s(dve.tensor_scalar(ng, ng, 1.0, None, ALU.add))
                s.sync()
                s(dve.reciprocal(ng, ng))
                dve.wait_ge(s_ln, 1)
                lf2 = lf.rearrange("p t h -> p (t h)")
                s(dve.tensor_scalar(lft[:, 2, :], lft[:, 0, :], 0.0, None, ALU.min))
                s.sync()
                dve.tensor_tensor(lf2, lft[:, 2, :], lft[:, 1, :], ALU.subtract).then_inc(s_lf, 1)
                dve.wait_ge(s_proj, L_KW + 1)
                for g in range(2):
                    for half in range(2):
                        dve.tensor_copy(nkT[1][DH * half:DH * half + DH, g, :], bank[2][DH * g:DH * g + DH, 0:T])
                dve.tensor_copy(nv[:, :, 1, :], two(bank[2])[:, 1, :].rearrange("p (t d) -> p t d", t=NT))\
                   .then_inc(s_evd, 1)
                Z, Q, E = cmpt[:, 0, :], cmpt[:, 1, :], cmpt[:, 2, :]
                Zb = Z.rearrange("p (v g n) -> p v g n", v=2, g=2)
                s(dve.memset(Z, 0.0))
                dve.wait_ge(s_hc, 1)
                for kv in range(2):
                    r = slice(64 * kv, 64 * kv + HROWS)
                    last = dve.tensor_copy(hrow[r, :], bank[4][r, 0:HID])
                last.then_inc(s_hcs, 1)
                dve.wait_ge(s_hct, 1)
                for kv in range(2):
                    s(dve.tensor_tensor(cmpt[:, 3, kv:kv + 1], bank[(4, 7)[kv]][:, T + 32:T + 33],
                                        b1[:, kv:kv + 1], ALU.add))
                s.sync()
                for kv in range(2):
                    s(dve.tensor_scalar(Zb[:, kv, :, 0:NCMP],
                                        bank[(4, 7)[kv]][:, T:T + 32].rearrange("p (g n) -> p g n", g=2)[:, :, 0:NCMP],
                                        cmpt[:, 3, kv:kv + 1], None, ALU.add))
                s.sync()
                s(dve.tensor_tensor(Q, Z, Z, ALU.mult))
                s.sync()
                s(dve.tensor_scalar(Q, Q, 0.044715, 1.0, ALU.mult, ALU.add))
                s.sync()
                dve.tensor_tensor(Q, Q, Z, ALU.mult).then_inc(s_gz, 1)
                dve.wait_ge(s_latp, 1)
                dve.tensor_tensor(cqT, two(bank[5]), bc(g_q, [P, 2, T]), ALU.mult).then_inc(s_latT, 1)
                dve.tensor_scalar(ckvT, bank[6][:, 0:T], g_kv, None, ALU.mult).then_inc(s_latT, 1)
                read(8, fqT[:, 2:4, :], two(bank[0]))
                dve.wait_ge(s_gexp, 1)
                s(dve.tensor_scalar(E, E, 1.0, None, ALU.add))
                s.sync()
                s(dve.reciprocal(E, E))
                s.sync()
                s(dve.tensor_tensor(hidc.rearrange("p a b -> p (a b)"), Z, E, ALU.mult))
                s.sync()
                for g in range(2):
                    last = dve.tensor_copy(hvr[:, 64 * g:64 * g + 64].rearrange("p (a n) -> p a n", a=4),
                                           hidc[:, 1, 16 * g:16 * g + 16].unsqueeze(1).broadcast_to([P, 4, 16]))
                last.then_inc(s_hid, 1)
                read(10, fkT[:, 2:4, :], two(bank[2]))
                dve.wait_ge(s_kv, 1)
                dve.tensor_copy(kcT, bank[7][:, 0:32])
                dve.tensor_tensor(vcbd, bank[7][:, 64:128].unsqueeze(1).broadcast_to([P, H, DH]),
                                  bc(cst[:, K_HM:K_HM + H], [P, H, DH]), ALU.mult).then_inc(s_kcT, 1)
                read(12, fv[:, :, 256:512], two(bank[0]))
                for i in range(4):
                    t, hf = divmod(i, 2)
                    dve.wait_ge(s_mq, i + 1)
                    s(dve.tensor_copy(qtm[:, t, 384 * hf:384 * hf + 384], bank[i][:, 0:384]))
                s.sync()
                qv = qtm.rearrange("p t (h d) -> p t h d", h=H)
                prod = [qrt[:, i, :].rearrange("p (t h c) -> p t h c", t=NT, h=H) for i in range(4)]
                for i, (lo, tr) in enumerate(((DH, 0), (DH + HALF, 1), (DH, 1), (DH + HALF, 0))):
                    for t in range(NT):
                        s(dve.tensor_tensor(prod[i][:, t], qv[:, t, :, lo:lo + HALF],
                                            trig[:, tr, t, :].unsqueeze(1).broadcast_to([P, H, HALF]), ALU.mult))
                s.sync()
                for t in range(NT):
                    s(dve.tensor_tensor(qv[:, t, :, DH:DH + HALF], prod[0][:, t], prod[1][:, t], ALU.subtract))
                    last = dve.tensor_tensor(qv[:, t, :, DH + HALF:QK], prod[2][:, t], prod[3][:, t], ALU.add)
                    if t == 0:
                        s(last)
                last.then_inc(s_qr, 1)
                dve.wait_ge(s_sc, 1)
                pcv = pc.rearrange("p t (c s n) -> p (t c) s n", s=2, n=16)
                bcv = biasc[:, :, :, :].rearrange("p t (c s) n -> p (t c) s n", s=2)
                for half in range(2):
                    s(dve.tensor_tensor(pcv[:, :, half, :], bank[5 + half][:, 0:128].rearrange("p (a n) -> p a n", n=16),
                                        bcv[:, :, half, :], ALU.add))
                s.sync()
                pch = pc.rearrange("p t (h n) -> p (t h) n", n=16)
                cm, cs = coef[:, 0:16], coef[:, 16:32]
                s(dve.tensor_reduce(cm, pch, AX.X, ALU.max))
                s.sync()
                dve.tensor_tensor(pch, pch, bc(cm, [P, 16, 16]), ALU.subtract).then_inc(s_sx, 1)
                dve.wait_ge(s_sexp, 1)
                s(dve.tensor_reduce(cs, pch, AX.X, ALU.add))
                s.sync()
                s(dve.reciprocal(cs, cs))
                s.sync()
                gates = ng.rearrange("p t (c s b) -> p t c s b", s=2, c=4)
                for t in range(NT):
                    s(dve.tensor_tensor(cs[:, 8 * t:8 * t + 8].rearrange("p (c s) -> p c s", s=2),
                                        cs[:, 8 * t:8 * t + 8].rearrange("p (c s) -> p c s", s=2),
                                        gates[:, t, :, :, 0], ALU.mult))
                    s(dve.tensor_tensor(pc[:, t, :].rearrange("p (h n) -> p h n", n=16),
                                        pc[:, t, :].rearrange("p (h n) -> p h n", n=16),
                                        cst[:, K_OK + 16 * t:K_OK + 16 * t + 16].unsqueeze(1).broadcast_to([P, H, 16]),
                                        ALU.mult))
                s.sync()
                dve.tensor_tensor(pch, pch, bc(cs, [P, 16, 16]), ALU.mult).then_inc(s_pc, 1)
                for i in range(4):
                    dve.wait_ge(s_fb, i + 1)
                    b = two(bank[(4, 7)[i % 2]])
                    mask = cst[:, K_MASK:K_MASK + T].unsqueeze(1).broadcast_to([P, 2, T])
                    dve.scalar_tensor_tensor(out=bias8[:, 2 * i:2 * i + 2, :], in0=b, scalar=-8.0, in1=mask,
                                             op0=ALU.mult, op1=ALU.add)
                    dve.scalar_tensor_tensor(out=bias0[:, 2 * i:2 * i + 2, :], in0=b[:, :, 0:P], scalar=-8.0,
                                             in1=mask[:, :, P:T], op0=ALU.mult, op1=ALU.add).then_inc(s_fbe, 1)

                def shifted(u):
                    br, c = divmod(u, 4)
                    dve.wait_ge(s_qk, u + 1)
                    if u == 0:
                        dve.wait_ge(s_fbe, 4)
                    if u == 4 * SLC:
                        dve.wait_ge(s_bias, 16)
                    if u >= 3:
                        dve.wait_ge(s_pt, 2 * u - 4)
                    for half in range(2):
                        h = 2 * c + half
                        for t in range(NT):
                            lo, hi = seg(t)
                            if br == MLA:
                                b = cst[:, K_MASK + P * (1 - t):K_MASK + T]
                            elif t == 1:
                                b = bias8[:, h, :]
                            else:
                                b = bias0[:, h, :] if br == FOX else bias8[:, h, P:T]
                            col = score_cols(u, t, half)
                            last = dve.tensor_tensor_reduce(
                                out=prob[u % 3][:, half, lo:hi], in0=bank[2 * (u % 2) + half][:, lo:hi], in1=b,
                                scale=1.0, scalar=-3e38, op0=ALU.add, op1=ALU.max, accum_out=mx[:, col:col + 1])
                            s(last)
                    s.sync()
                    m = mx[:, 8 * (u // 2):8 * (u // 2) + 8].rearrange("p (t v s) -> p t v s", t=NT, s=2)[:, :, u % 2, :]
                    scale = QK ** -0.5 if br == MLA else DH ** -0.5
                    dve.tensor_scalar(m, m, -scale, None, ALU.mult).then_inc(s_max, 1)

                def read_out(g):
                    br, gg = divmod(g, 2)
                    dve.wait_ge(s_pv, 2 * g + 2)
                    if g == 2 * SLC:
                        dve.wait_ge(s_oce, 2)
                    r = coef[:, 8 * g:8 * g + 8]
                    s(dve.reciprocal(r, sm[:, 8 * g:8 * g + 8]))
                    s.sync()
                    if br >= SLC:
                        for t in range(NT):
                            rt = r[:, 4 * t:4 * t + 4].rearrange("p (c s) -> p c s", s=2)
                            s(dve.tensor_tensor(rt, rt, gates[:, t, 2 * gg:2 * gg + 2, :, br - SLC + 1], ALU.mult))
                        s.sync()
                    o = bank[6 + g % 2][:, :].rearrange("p (a d) -> p a d", d=DH)
                    acc = (of_, om_, on_, on_)[br][:, :, 256 * gg:256 * gg + 256]
                    if br < SLC:
                        dst = acc.rearrange("p t (i d) -> p t i d", d=DH)
                        for t in range(NT):
                            last = dve.tensor_tensor(dst[:, t], o[:, 4 * t:4 * t + 4, :],
                                                     bc(r[:, 4 * t:4 * t + 4], [P, 4, DH]), ALU.mult)
                        last.then_inc(s_oe, 1)
                    else:
                        s(dve.tensor_tensor(otmp.rearrange("p (a d) -> p a d", d=DH), o, bc(r, [P, 8, DH]), ALU.mult))
                        s.sync()
                        dve.tensor_tensor(acc, acc, otmp.rearrange("p (t c) -> p t c", t=NT), ALU.add)\
                           .then_inc(s_oe, 1)
                        dve.wait_ge(s_oe, g + 1)

                for u in range(UNITS + 3):
                    if u < UNITS:
                        shifted(u)
                    if u >= 4 and u % 2 == 0:
                        read_out((u - 4) // 2)
                for n, i in ((0, 2), (2, 4), (4, 0)):
                    dve.wait_ge(s_ot, n + 1)
                    dve.tensor_copy(oT[:, i // 2, 0:2, :], two(bank[4 + n % 3])).then_inc(s_oTe, 1)
                for q in range(24):
                    m, b = divmod(q, 3)
                    e = mexp[:, q % 4, :]
                    dve.wait_ge(s_mge, q + 1)
                    s(dve.tensor_scalar(e, e, 1.0, None, ALU.add))
                    s.sync()
                    s(dve.reciprocal(e, e))
                    s.sync()
                    dve.wait_ge(s_mg, q + 1)
                    if b == 0:
                        dve.tensor_tensor(mixT[:, m, :], e, bank[4 + q % 4][:, 0:T], ALU.mult).then_inc(s_mgd, 1)
                    else:
                        s(dve.tensor_tensor(mtmp[:, q % 2, :], e, bank[4 + q % 4][:, 0:T], ALU.mult))
                        s.sync()
                        dve.wait_ge(s_mgd, q)
                        dve.tensor_tensor(mixT[:, m, :], mixT[:, m, :], mtmp[:, q % 2, :], ALU.add).then_inc(s_mgd, 1)
                for i in range(4):
                    dve.wait_ge(s_op, i + 1)
                    xi = x[:, :, 256 * i:256 * i + 256]
                    dve.tensor_tensor(xi, xi, two(bank[4 + i]), ALU.add)

        with nc.Block() as block:
            TURNED = ((0, 0), (0, 1), (1, 1), (1, 0))

            def got(eng, j, c):
                slot, turn = c % MOE_SLOTS, c // MOE_SLOTS
                if slot < SLOTS:
                    eng.wait_ge(landed[slot], (layer * TURNS + j * 3 + (ATT_TURNS + turn + 1)) * 16)
                else:
                    eng.wait_ge(landed[slot], (layer * MOE_TURNS + j * 3 + (turn + 1)) * 16)

            def moe_slot(c, n=1):
                slot = c % MOE_SLOTS
                return ring[:, slot:slot + n, :] if slot < SLOTS else spare[:, slot - SLOTS:slot - SLOTS + n, :]

            @block.sync
            def _(sp):
                def load(j, c):
                    e, m = GROUP[c % 12]
                    expert_load(sp, layer, j * 16 + (4 * (c // 12) + e), m, moe_slot(c)[:, 0, :], landed[c % MOE_SLOTS])

                for c in range(SLOTS, MOE_SLOTS):
                    load(0, c)

                def refill(j, c):
                    g, i = divmod(c - MOE_SLOTS, 12)
                    if i == 0:
                        sp.wait_ge(s_gu, j * 4 + (g + 1))
                    if i == 8:
                        sp.wait_ge(s_y, j * 8 + (2 * g + 3))
                    load(j, c)

                with sp.Fori(0, NGRP // 4 - 1) as j:
                    for c in range(MOE_SLOTS, 48 + MOE_SLOTS):
                        refill(j, c)
                for c in range(MOE_SLOTS, 48):
                    refill(NGRP // 4 - 1, c)
                with sp.If(layer < DEPTH - 1):
                    sp.wait_ge(s_y, 2 * NGRP - 1)
                    for n in range(AHEAD):
                        if n == 4:
                            sp.wait_ge(s_gu, NGRP)
                        attention_load(sp, DEPTH - 1, n)

            @block.gpsimd
            def _(pool):
                g = Chain(pool, s_gc2)
                pool.memset(ysb, 0.0).then_inc(s_yz, 1)
                norm_pool(pool, g, 1)
                pool.wait_ge(s_rstd, 2)
                g(pool.memset(Ssel[:, :, NGRP, :], 0.0))
                g.sync()
                g(pool.memset(STw[:, 0, :], 0.0))
                g.sync()
                for t in range(NT):
                    pool.wait_ge(s_S, t + 1)
                    pool.tensor_tensor(Sw[:, t], picked(t), bc(Wsel[:, t, :], [P, NE, CAP]), ALU.mult).then_inc(s_sw, 1)

            @block.tensor
            def _(pe):
                norm_tensor(pe, x)
                pe.wait_ge(s_wr, 64)
                for k in range(KD):
                    if k % 2 == 0:
                        norm_ready(pe, k, 1)
                    for t in range(NT):
                        last = pe.matmul(bank[4][:, t * 64:t * 64 + NG + NE], hT[:, k, t * P:(t + 1) * P], wrt[:, k, :],
                                         start=(k == 0 and t == 0), stop=(k == KD - 1), skip_group_check=True)
                last.then_inc(s_lg, 1)
                pe.wait_ge(s_yz, 1)
                zeros = ysb[:, 0, :].bitcast(mybir.dt.bfloat16)
                for b in range(4 * 8):
                    pe.matmul(bank[b % 4][:, :], zeros[:, 0:P], zeros[:, 0:512], start=True, stop=False,
                              skip_group_check=True)
                pe.wait_ge(s_sel, 1)
                strict, ones = cst[:, K_STRICT:K_STRICT + P], cst[:, K_ONES:K_ONES + P]
                pe.matmul(bank[5][:, 0:NE], strict, Msel[:, 0, :], start=True, stop=True)
                pe.matmul(bank[5][:, NE:2 * NE], ones, Msel[:, 0, :], start=True, stop=False)
                pe.matmul(bank[5][:, NE:2 * NE], strict, Msel[:, 1, :], start=False, stop=True)
                pe.matmul(bank[5][:, 2 * NE:3 * NE], ones, Msel[:, 0, :], start=True, stop=False)
                pe.matmul(bank[5][:, 2 * NE:3 * NE], ones, Msel[:, 1, :], start=False, stop=True).then_inc(s_rk, 1)

                def gather(sel):
                    for half in range(2):
                        b = bank[7 - half]
                        for a in range(4):
                            for t in range(NT):
                                last = pe.matmul(b[:, a * P:(a + 1) * P], h2[:, t, 4 * half + a::KD], sel(t),
                                                 start=(t == 0), stop=(t == NT - 1))
                        last.then_inc(s_xg, 1)

                for b in range(4 * 4):
                    pe.matmul(bank[b % 4][:, :], zeros[:, 0:P], zeros[:, 0:512], start=True, stop=False,
                              skip_group_check=True)
                pe.wait_ge(s_S, 2)
                gather(lambda t: Ssel[:, t, 0, :])
                for n, (t, r) in enumerate(TURNED):
                    pe.wait_ge(s_sw, t + 1)
                    if n == 1:
                        pe.wait_ge(s_xge, 2)
                    if n == 3:
                        pe.wait_ge(s_sta, 1)
                    for a in range(4):
                        last = pe.transpose(bank[(5, 6, 7, 5)[n]][:, a * P:(a + 1) * P],
                                            Sw[:, t, 4 * (4 * r + a):4 * (4 * r + a) + 4, :].rearrange("p e c -> p (e c)"),
                                            ident)
                    last.then_inc(s_st, 1)

                def scatter(q, rhs, chunks=range(KD)):
                    for m in chunks:
                        last = pe.matmul(bank[m // 2][:, (m % 2) * T:(m % 2 + 1) * T], ysb[:, q, m * P:(m + 1) * P], rhs,
                                         start=False, stop=False, skip_group_check=True)
                    return last

                for first_use in (s_scat, s_hdt, s_y):
                    pe.sem_inc(first_use, 1)
                with pe.Fori(0, NGRP // 4) as j:
                    for g in range(4):
                        q = g % 2
                        pe.wait_ge(s_xge, j * 8 + (2 * g + 2))
                        pe.wait_ge(s_hde, j * 4 + (g + 1))
                        for i in range(8):
                            got(pe, j, 12 * g + i)
                        for k in range(KD):
                            for e in range(4):
                                w = moe_slot(12 * g + 2 * e, 2)[:, :, k * F:(k + 1) * F]
                                last = pe.matmul(bank[4][CAP * e:CAP * e + CAP, :].rearrange("p (a f) -> p a f", a=2),
                                                 XT[:, q, k, CAP * e:CAP * e + CAP], w,
                                                 start=(k == 0), stop=(k == KD - 1))
                        last.then_inc(s_gu, 1)
                        pe.wait_ge(s_std, 2)
                        pe.wait_ge(s_sta, 2)
                        pe.wait_ge(s_ye, j * 8 + (2 * g + 1))
                        gather(lambda t: Ssel[:, t, j * 4 + (g + 1), :])
                        pe.wait_ge(s_hd, j * 4 + (g + 2))
                        for a in range(2):
                            last = pe.transpose(bank[4][:, a * P:(a + 1) * P], hid[:, 2, a::2], ident)
                        last.then_inc(s_hdt, 1)
                        scatter(1 - q, STw[:, j * 4 + g, :]).then_inc(s_scat, 1)
                        pe.wait_ge(s_hde, j * 4 + (g + 2))
                        for i in range(8, 12):
                            got(pe, j, 12 * g + i)
                        for n in range(2):
                            if n == 1:
                                pe.wait_ge(s_xge, j * 8 + (2 * g + 4))
                            for a in range(2):
                                for e in range(4):
                                    last = pe.matmul(bank[5 + n][CAP * e:CAP * e + CAP, :],
                                                     hidT[:, a, CAP * e:CAP * e + CAP],
                                                     moe_slot(12 * g + 8 + e)[:, 0, a * D + 512 * n:a * D + 512 * n + 512],
                                                     start=(a == 0), stop=(a == 1))
                            last.then_inc(s_y, 1)
                for r in range(2):
                    pe.wait_ge(s_ye, 2 * NGRP + r)
                    scatter(1, STw[:, NGRP, :], range(4 * r, 4 * r + 4)).then_inc(s_acc, 1)
                for r in range(2):
                    pe.wait_ge((s_acd, s_aca)[r], 2)
                    for t in range(NT):
                        for a in range(4):
                            last = pe.transpose(bank[4 + 2 * r + t][:, a * P:(a + 1) * P],
                                                accsb[:, 4 * r + a, t * P:(t + 1) * P], ident)
                        last.then_inc(s_fin, 1)

            @block.scalar
            def _(act):
                norm_scalar(act)
                norm_read_scalar(act, g_ffn, 1)
                act.wait_ge(s_rx, 1)
                act.activation(lgp[:, :, 0:NG], lgp[:, :, 0:NG], ACT.Exp).then_inc(s_rxe, 1)
                act.wait_ge(s_rx, 2)
                act.activation(rw[:, 4:6], rw[:, 2:4], ACT.Exp).then_inc(s_rxe, 1)
                for n in (0, 3):
                    t, r = TURNED[n]
                    act.wait_ge(s_st, n + 1)
                    act.activation(STw[:, 1 + 4 * r:5 + 4 * r, t * P:(t + 1) * P],
                                   bank[5][:, :].rearrange("p (a c) -> p a c", a=4), ACT.Copy).then_inc(s_sta, 1)
                act.wait_ge(s_yz, 1)
                act.sem_inc(s_ye, 1)
                with act.Fori(0, NGRP // 4) as j:
                    for g in range(4):
                        q = g % 2
                        act.wait_ge(s_gu, j * 4 + (g + 1))
                        act.wait_ge(s_hd, j * 4 + (g + 1))
                        act.activation(hid[:, 0, :], bank[4][:, 0:F], ACT.Exp, scale=-1.0).then_inc(s_ge, 1)
                        act.wait_ge(s_scat, j * 4 + (g + 1))
                        for n in range(2):
                            act.wait_ge(s_y, j * 8 + (2 * g + n + 1 + 1))
                            act.activation(ysb[:, q, 512 * n:512 * n + 512], bank[5 + n][:, :], ACT.Copy)\
                               .then_inc(s_ye, 1)
                act.wait_ge(s_acc, 2)
                for b in (2, 3):
                    act.activation(accsb[:, 2 * b:2 * b + 2, :], bank[b][:, :].rearrange("p (a t) -> p a t", a=2), ACT.Copy)\
                       .then_inc(s_aca, 1)

            @block.vector
            def _(dve):
                s = Chain(dve, s_dc2)
                norm_square(dve, s_ss)
                norm_read_vector(dve, g_ffn, 1)
                s(dve.memset(lgp[:, :, NG:], -3e38))
                norm_vector(dve, 1)
                dve.wait_ge(s_wr, 64)
                dve.wait_ge(s_lg, 1)
                for t in range(NT):
                    s(dve.scalar_tensor_tensor(out=lg[:, t, :], in0=bank[4][:, 64 * t:64 * t + NG + NE],
                                               scalar=rstd[:, t:t + 1], in1=rb, op0=ALU.mult, op1=ALU.add))
                s.sync()
                s(dve.tensor_copy(lgp[:, :, 0:NG], lg[:, :, 0:NG]))
                s.sync()
                for t in range(NT):
                    s(dve.max(t8[:, t, :], lgp[:, t, :]))
                s.sync()
                for t in range(NT):
                    s(dve.max_index(i8[:, t, :].bitcast(U32), t8[:, t, :], lgp[:, t, :]))
                s.sync()
                for t in range(NT):
                    s(dve.tensor_copy(gf[:, t:t + 1], i8[:, t, 0:1].bitcast(U32)))
                    last = dve.tensor_scalar(lgp[:, t, 0:NG], lg[:, t, 0:NG], t8[:, t, 0:1], None, ALU.subtract)
                    if t == 0:
                        s(last)
                last.then_inc(s_rx, 1)
                s.sync()
                for t in range(NT):
                    s(dve.tensor_scalar(el[:, t, :], cst[:, K_GRP:K_GRP + NE], gf[:, t:t + 1], -BIG,
                                        ALU.not_equal, ALU.mult))
                s.sync()
                s(dve.tensor_tensor(el, el, lg[:, :, NG:], ALU.add))
                s.sync()
                for t in range(NT):
                    s(dve.max(t8[:, t, :], el[:, t, :]))
                s.sync()
                for t in range(NT):
                    s(dve.max_index(i8[:, t, :].bitcast(U32), t8[:, t, :], el[:, t, :]))
                s.sync()
                for t in range(NT):
                    s(dve.tensor_copy(gf[:, 2 + 2 * t:4 + 2 * t], i8[:, t, 0:2].bitcast(U32)))
                    last = dve.tensor_tensor(rw[:, 2 + t:3 + t], t8[:, t, 1:2], t8[:, t, 0:1], ALU.subtract)
                    if t == 0:
                        s(last)
                last.then_inc(s_rx, 1)
                dve.wait_ge(s_rxe, 1)
                s(dve.tensor_reduce(rw[:, 0:2], lgp[:, :, 0:NG], AX.X, ALU.add))
                dve.wait_ge(s_rxe, 2)
                s(dve.tensor_scalar(rw[:, 6:8], rw[:, 4:6], 1.0, None, ALU.add))
                s.sync()
                s(dve.tensor_tensor(rw[:, 6:8], rw[:, 6:8], rw[:, 0:2], ALU.mult))
                s.sync()
                s(dve.reciprocal(rw[:, 8:10], rw[:, 6:8]))
                s.sync()
                s(dve.tensor_tensor(rw[:, 10:12], rw[:, 8:10], rw[:, 4:6], ALU.mult))
                for t in range(NT):
                    for a in range(2):
                        s(dve.tensor_scalar(oh[:, a, :], cst[:, K_IOTA:K_IOTA + NE], gf[:, 2 + 2 * t + a:3 + 2 * t + a],
                                            None, ALU.is_equal))
                    s.sync()
                    s(dve.tensor_tensor(Msel[:, t, :], oh[:, 0, :], oh[:, 1, :], ALU.add))
                    s(dve.tensor_scalar(Wsel[:, t, :], oh[:, 0, :], rw[:, 8 + t:9 + t], None, ALU.mult))
                    s.sync()
                    last = dve.scalar_tensor_tensor(out=Wsel[:, t, :], in0=oh[:, 1, :], scalar=rw[:, 10 + t:11 + t],
                                                    in1=Wsel[:, t, :], op0=ALU.mult, op1=ALU.add)
                    if t == 0:
                        s(last)
                        s.sync()
                last.then_inc(s_sel, 1)
                dve.wait_ge(s_sel, 1)
                dve.wait_ge(s_rk, 1)
                s(dve.tensor_scalar(Rk, bank[5][:, 0:2 * NE].rearrange("p (t e) -> p t e", t=NT), 1.0, None, ALU.add))
                s.sync()
                s(dve.tensor_tensor(Rk, Rk, Msel, ALU.mult))
                s.sync()
                s(dve.tensor_scalar(Rk, Rk, -1.0, None, ALU.add))
                s(dve.tensor_reduce(cmax[:, 0:1], bank[5][:, 2 * NE:3 * NE], AX.X, ALU.max))
                s.sync()
                dve.tensor_scalar(ovf[:, :], cmax[:, 0:1], float(CAP), None, ALU.is_gt)
                slots = cst[:, K_IOTA:K_IOTA + CAP].unsqueeze(1).broadcast_to([P, NE, CAP])

                for t in range(NT):
                    dve.tensor_tensor(picked(t), slots, bc(Rk[:, t, :], [P, NE, CAP]), ALU.is_equal).then_inc(s_S, 1)

                def gathered(half, q):
                    dve.tensor_tensor(XT[:, q, 4 * half:4 * half + 4, :], bank[7 - half][:, :].rearrange("p (a c) -> p a c", a=4),
                                      bc(g_ffn[:, 4 * half:4 * half + 4], [P, 4, P]), ALU.mult).then_inc(s_xge, 1)

                for half in range(2):
                    dve.wait_ge(s_xg, half + 1)
                    gathered(half, 0)
                for n in (1, 2):
                    t, r = TURNED[n]
                    dve.wait_ge(s_st, n + 1)
                    dve.tensor_copy(STw[:, 1 + 4 * r:5 + 4 * r, t * P:(t + 1) * P],
                                    bank[5 + n][:, :].rearrange("p (a c) -> p a c", a=4)).then_inc(s_std, 1)
                for first_use in (s_hde, s_hd):
                    dve.sem_inc(first_use, 1)
                with dve.Fori(0, NGRP // 4) as j:
                    for g in range(4):
                        q = g % 2
                        s2 = Chain(dve, s_dch)
                        dve.sem_clear(s_dch)
                        dve.wait_ge(s_ge, j * 4 + (g + 1))
                        s2(dve.tensor_scalar(hid[:, 0, :], hid[:, 0, :], 1.0, None, ALU.add))
                        s2.sync()
                        s2(dve.reciprocal(hid[:, 1, :], hid[:, 0, :]))
                        s2.sync()
                        s2(dve.tensor_tensor(hid[:, 1, :], hid[:, 1, :], bank[4][:, 0:F], ALU.mult))
                        s2.sync()
                        dve.wait_ge(s_hdt, j * 4 + (g + 1))
                        dve.tensor_tensor(hid[:, 2, :], hid[:, 1, :], bank[4][:, F:2 * F], ALU.mult).then_inc(s_hd, 1)
                        dve.wait_ge(s_hdt, j * 4 + (g + 2))
                        dve.wait_ge(s_y, j * 8 + (2 * g + 1))
                        dve.tensor_copy(hidT, bank[4][:, 0:2 * P].rearrange("p (a c) -> p a c", a=2)).then_inc(s_hde, 1)
                        for half in range(2):
                            dve.wait_ge(s_xg, j * 8 + (2 * g + 3 + half))
                            gathered(half, 1 - q)
                dve.wait_ge(s_acc, 1)
                for b in (0, 1):
                    dve.tensor_copy(accsb[:, 2 * b:2 * b + 2, :], bank[b][:, :].rearrange("p (a t) -> p a t", a=2))\
                       .then_inc(s_acd, 1)
                for i in range(4):
                    r, t = divmod(i, 2)
                    dve.wait_ge(s_fin, i + 1)
                    xi = x[:, t, 512 * r:512 * r + 512]
                    dve.tensor_tensor(xi, xi, bank[4 + i][:, :], ALU.add)

        over = nc.values_load(ovf[0:1, 0:1], min_val=0, max_val=1)
        with nc.If(over > 0):
            (o_sel, o_xg, o_xge, o_gu, o_ge, o_hd, o_hdt, o_hde, o_y, o_ye, o_st, o_wt, o_wte, o_sum) = s_o
            over_sems = range(s_ow.num, s_o[-1].num + 1)
            XO = XT[:, 0, :, 0:CAP]
            with nc.Fori(1, PASSES):
                with nc.Block() as block:
                    @block.vector
                    def _(dve):
                        s = Chain(dve, o_st)
                        s(dve.tensor_scalar(Rk, Rk, -float(CAP), None, ALU.add))
                        s(dve.tensor_scalar(cmax[:, 0:1], cmax[:, 0:1], -float(CAP), None, ALU.add))
                        s.sync()
                        dve.tensor_scalar(left[:, :], cmax[:, 0:1], 0.0, None, ALU.is_gt)
                nc.multi_engine_barrier(ALL, sems_to_clear=over_sems)
                more = nc.values_load(left[0:1, 0:1], min_val=0, max_val=1)
                with nc.If(more > 0):
                    with nc.Fori(0, NE) as ex:
                        with nc.Block() as block:
                            @block.sync
                            def _(sp):
                                for i in range(3):
                                    expert_load(sp, layer, ex, i, ovw[:, i, :], s_ow)

                            @block.vector
                            def _(dve):
                                s = Chain(dve, o_st)
                                for t in range(NT):
                                    s(dve.tensor_scalar(ovS[:, t, :], cst[:, K_IOTA:K_IOTA + CAP], Rk[:, t, bass.ds(ex, 1)],
                                                        None, ALU.is_equal))
                                s.sync()
                                for t in range(NT):
                                    dve.tensor_scalar(ovW[:, t, :], ovS[:, t, :], Wsel[:, t, bass.ds(ex, 1)], None,
                                                      ALU.mult).then_inc(o_sel, 1)
                                dve.wait_ge(o_xg, 1)
                                dve.tensor_tensor(XO, bank[0][:, 0:KD * CAP].rearrange("p (a c) -> p a c", a=KD),
                                                  bc(g_ffn, [P, KD, CAP]), ALU.mult).then_inc(o_xge, 1)
                                dve.wait_ge(o_wt, 1)
                                dve.tensor_copy(ovT[0:CAP, :], bank[5][0:CAP, 0:T]).then_inc(o_wte, 1)
                                dve.wait_ge(o_ge, 1)
                                s(dve.tensor_scalar(hid[0:CAP, 0, :], hid[0:CAP, 0, :], 1.0, None, ALU.add))
                                s.sync()
                                s(dve.reciprocal(hid[0:CAP, 1, :], hid[0:CAP, 0, :]))
                                s.sync()
                                s(dve.tensor_tensor(hid[0:CAP, 1, :], hid[0:CAP, 1, :], bank[1][0:CAP, 0:F], ALU.mult))
                                s.sync()
                                dve.tensor_tensor(hid[0:CAP, 2, :], hid[0:CAP, 1, :], bank[1][0:CAP, F:2 * F],
                                                  ALU.mult).then_inc(o_hd, 1)
                                dve.wait_ge(o_hdt, 1)
                                dve.tensor_copy(hidT[:, :, 0:CAP], bank[2][:, 0:2 * CAP].rearrange("p (a c) -> p a c", a=2))\
                                   .then_inc(o_hde, 1)
                                for i in range(4):
                                    t, n = divmod(i, 2)
                                    dve.wait_ge(o_sum, i + 1)
                                    xi = x[:, t, 512 * n:512 * n + 512]
                                    dve.tensor_tensor(xi, xi, bank[(6, 7, 0, 1)[i]][:, :], ALU.add)

                            @block.scalar
                            def _(act):
                                act.wait_ge(o_gu, 1)
                                act.activation(hid[0:CAP, 0, :], bank[1][0:CAP, 0:F], ACT.Exp, scale=-1.0).then_inc(o_ge, 1)
                                for n in range(2):
                                    act.wait_ge(o_y, n + 1)
                                    act.activation(ysb[0:CAP, 0, 512 * n:512 * n + 512], bank[3 + n][0:CAP, :], ACT.Copy)\
                                       .then_inc(o_ye, 1)

                            @block.tensor
                            def _(pe):
                                pe.wait_ge(o_sel, 2)
                                for k in range(KD):
                                    for t in range(NT):
                                        last = pe.matmul(bank[0][:, k * CAP:(k + 1) * CAP], h2[:, t, k::KD], ovS[:, t, :],
                                                         start=(t == 0), stop=(t == NT - 1))
                                last.then_inc(o_xg, 1)
                                for t in range(NT):
                                    last = pe.transpose(bank[5][0:CAP, t * P:(t + 1) * P], ovW[:, t, :], ident)
                                last.then_inc(o_wt, 1)
                                pe.wait_ge(s_ow, 48)
                                pe.wait_ge(o_xge, 1)
                                for k in range(KD):
                                    last = pe.matmul(bank[1][0:CAP, :].rearrange("p (a f) -> p a f", a=2), XO[:, k, :],
                                                     ovw[:, 0:2, k * F:(k + 1) * F], start=(k == 0), stop=(k == KD - 1))
                                last.then_inc(o_gu, 1)
                                pe.wait_ge(o_hd, 1)
                                for a in range(2):
                                    last = pe.transpose(bank[2][:, a * CAP:(a + 1) * CAP], hid[0:CAP, 2, a::2],
                                                        ident[0:CAP, 0:CAP])
                                last.then_inc(o_hdt, 1)
                                pe.wait_ge(o_hde, 1)
                                for n in range(2):
                                    for a in range(2):
                                        last = pe.matmul(bank[3 + n][0:CAP, :], hidT[:, a, 0:CAP],
                                                         ovw[:, 2, a * D + 512 * n:a * D + 512 * n + 512],
                                                         start=(a == 0), stop=(a == 1))
                                    last.then_inc(o_y, 1)
                                pe.wait_ge(o_ye, 2)
                                pe.wait_ge(o_wte, 1)
                                for i in range(4):
                                    t, n = divmod(i, 2)
                                    pe.matmul(bank[(6, 7, 0, 1)[i]][:, :], ovT[0:CAP, t * P:(t + 1) * P],
                                              ysb[0:CAP, 0, 512 * n:512 * n + 512], start=True, stop=True).then_inc(o_sum, 1)
                        nc.multi_engine_barrier(ALL, sems_to_clear=over_sems)
                nc.multi_engine_barrier(ALL, sems_to_clear=over_sems)
        nc.multi_engine_barrier(ALL, sems_to_clear=layer_sems)

    gfin = region(4096, D)
    f_ld = sem("final_gain_loaded")
    f_ss = sem("final_squares")
    f_st = sem("final_steps")
    f_rs = sem("final_rstd")
    f_o = sem("final_ready")
    with nc.Block() as block:
        @block.sync
        def _(sp):
            sp.dma_start(gfin, A["norm_final"].partition_broadcast(P)).then_inc(f_ld, 16)
            for t in range(NT):
                sp.wait_ge(f_o, t + 1)
                sp.dma_start(out[0, t * P:(t + 1) * P, :], hA[:, t, :]).then_inc(stored, 16)
            sp.wait_ge(stored, 16 * NT)

        @block.scalar
        def _(act):
            act.activation(hA[:, 0, :], x[:, 0, :], ACT.Square, accum_out=ss[:, 0:1]).then_inc(f_ss, 1)

        @block.gpsimd
        def _(pool):
            g = Chain(pool, f_st)
            pool.wait_ge(f_ss, NT)
            g(pool.tensor_scalar(ss[:, 2:4], ss[:, 0:2], 1.0 / D, EPS, ALU.mult, ALU.add))
            g.sync()
            pool.tensor_tensor(rstd[:, 0:2], ss[:, 2:4], rexp[:, 0:2], ALU.pow).then_inc(f_rs, 1)

        @block.vector
        def _(dve):
            norm_square(dve, f_ss)
            dve.wait_ge(f_rs, 1)
            dve.wait_ge(f_ld, 16)
            for t in range(NT):
                dve.scalar_tensor_tensor(out=hA[:, t, :], in0=x[:, t, :], scalar=rstd[:, t:t + 1], in1=gfin,
                                         op0=ALU.mult, op1=ALU.mult).then_inc(f_o, 1)


_INS = ["x", "positions", "rel_bias", "norm_attn", "w_in", "b_merge", "cmp_pe", "cmp_k_w1", "cmp_k_b1", "cmp_k_w2",
        "cmp_v_w1", "cmp_v_b1", "cmp_v_w2", "mla_q_norm", "mla_kv_norm", "mla_w_uq", "mla_w_uk", "mla_w_uv", "fox_b_f",
        "w_o_nsa", "w_o_mla", "w_o_fox", "w_out", "norm_ffn", "moe_w_grp", "moe_b_grp", "moe_w_router",
        "moe_b_router", "moe_w_gate", "moe_w_up", "moe_w_down", "norm_final"]


def kernel(**inputs):
    import concourse.bacc as bacc
    from concourse.bass_utils import run_bass_kernel_spmd

    nc = bacc.Bacc("TRN2", target_bir_lowering=False, num_devices=1)
    arrays, aps = {}, {}
    consts = shape_constants()
    for name, a in [(n, inputs[n]) for n in _INS] + [("shape_c", consts[0]), ("shape_oh", consts[1])]:
        a = np.ascontiguousarray(a)
        arrays[f"in_{name}"] = a
        aps[name] = nc.dram_tensor(f"in_{name}", a.shape, mybir.dt.from_np(a.dtype), kind="ExternalInput").ap()
    out = nc.dram_tensor("out_0", (1, T, D), F32, kind="ExternalOutput").ap()
    build(nc, aps, out)
    r = run_bass_kernel_spmd(nc, [arrays], core_ids=[0])
    return r.results[0]["out_0"]
```
